# Optimizing a Trainium2 kernel written in Bass

```python
import math
import jax, jax.numpy as jnp
from jax import lax
import numpy as np

D_MODEL = 1024
BATCH = 1
SEQ = 512
DEPTH = 1

N_MEM = 256
D_RNN = D_MODEL
N_LRU_HEADS = 8
LRU_BLOCK = D_RNN // N_LRU_HEADS
LRU_CONV = 4
LRU_C = 8.0
D_CONV = D_MODEL
SC_CONV = 3
N_XHEADS = 4
XHEAD_DIM = D_MODEL // N_XHEADS
D_FF = 3 * D_MODEL
FFN_CONV = 3
LN_EPS = 1e-5
DN_ALPHA = (2.0 * DEPTH) ** 0.25
DN_BETA = (8.0 * DEPTH) ** -0.25
IN_SPLITS = [D_RNN, D_RNN, D_CONV, D_CONV, D_CONV, D_MODEL, D_MODEL]
IN_COLS = sum(IN_SPLITS)

kernel_name = "hawk_shortconv_gated_hybrid_deepnorm"

def layer_norm(x, g, b):
    xf = x.astype(jnp.float32)
    mu = jnp.mean(xf, axis=-1, keepdims=True)
    var = jnp.mean(jnp.square(xf - mu), axis=-1, keepdims=True)
    y = (xf - mu) * lax.rsqrt(var + LN_EPS)
    return (y * g.astype(jnp.float32) + b.astype(jnp.float32)).astype(x.dtype)

def causal_dwconv(u, w):
    k_width = w.shape[0]
    s = u.shape[1]
    up = jnp.pad(u, ((0, 0), (k_width - 1, 0), (0, 0)))
    return sum(up[:, k_width - 1 - k: k_width - 1 - k + s] * w[k] for k in range(k_width))

def block_diag_linear(u, w, b):
    bsz, s, d = u.shape
    uh = u.reshape(bsz, s, w.shape[0], w.shape[1])
    return jnp.einsum('bshi,hij->bshj', uh, w).reshape(bsz, s, d) + b

def rg_lru(u, w_r, b_r, w_i, b_i, lam):
    s = u.shape[1]
    r = jax.nn.sigmoid(block_diag_linear(u, w_r, b_r).astype(jnp.float32))
    i = jax.nn.sigmoid(block_diag_linear(u, w_i, b_i).astype(jnp.float32))
    log_a = -LRU_C * r * jax.nn.softplus(-lam.astype(jnp.float32))
    a = jnp.exp(log_a)
    mult = jnp.sqrt(-jnp.expm1(2.0 * log_a))
    is_first = (jnp.arange(s) == 0)[None, :, None]
    mult = jnp.where(is_first, 1.0, mult)
    bterm = mult * (i * u.astype(jnp.float32))

    def combine(left, right):
        a_l, b_l = left
        a_r, b_r_ = right
        return a_l * a_r, a_r * b_l + b_r_

    _, h = lax.associative_scan(combine, (a, bterm), axis=1)
    return h.astype(u.dtype)

def setup_inputs(seed: int = 0) -> dict:
    key = jax.random.key(seed)
    ks = iter(jax.random.split(key, 40))

    def nrm(shape, scale):
        return jax.random.normal(next(ks), shape, jnp.float32) * scale

    def gain(shape):
        return 1.0 + nrm(shape, 0.02)

    L = DEPTH
    x = nrm((BATCH, SEQ, D_MODEL), 1.0)
    mem = nrm((BATCH, N_MEM, D_MODEL), 1.0)
    a_c = jax.random.uniform(next(ks), (L, D_RNN), jnp.float32, 0.9, 0.999)
    p = a_c ** (1.0 / LRU_C)
    lru_lambda = jnp.log(p) - jnp.log1p(-p)
    return {
        "x": x,
        "mem": mem,
        "w_in": nrm((L, D_MODEL, IN_COLS), D_MODEL ** -0.5),
        "lru_conv_w": nrm((L, LRU_CONV, D_RNN), LRU_CONV ** -0.5),
        "lru_conv_b": nrm((L, D_RNN), 0.02),
        "w_rgate": nrm((L, N_LRU_HEADS, LRU_BLOCK, LRU_BLOCK), LRU_BLOCK ** -0.5),
        "b_rgate": nrm((L, D_RNN), 0.02),
        "w_igate": nrm((L, N_LRU_HEADS, LRU_BLOCK, LRU_BLOCK), LRU_BLOCK ** -0.5),
        "b_igate": nrm((L, D_RNN), 0.02),
        "lru_lambda": lru_lambda,
        "w_lru_out": nrm((L, D_RNN, D_MODEL), DN_BETA * D_RNN ** -0.5),
        "sc_conv_w": nrm((L, SC_CONV, D_CONV), SC_CONV ** -0.5),
        "w_sc_out": nrm((L, D_CONV, D_MODEL), DN_BETA * D_CONV ** -0.5),
        "b_merge": nrm((L, 2, D_MODEL), 0.02),
        "w_mix_out": nrm((L, D_MODEL, D_MODEL), DN_BETA * D_MODEL ** -0.5),
        "ln1_g": gain((L, D_MODEL)),
        "ln1_b": nrm((L, D_MODEL), 0.02),
        "w_q": nrm((L, D_MODEL, D_MODEL), D_MODEL ** -0.5),
        "w_k": nrm((L, D_MODEL, D_MODEL), D_MODEL ** -0.5),
        "w_v": nrm((L, D_MODEL, D_MODEL), DN_BETA * D_MODEL ** -0.5),
        "w_xo": nrm((L, D_MODEL, D_MODEL), DN_BETA * D_MODEL ** -0.5),
        "ln2_g": gain((L, D_MODEL)),
        "ln2_b": nrm((L, D_MODEL), 0.02),
        "w_ffn_gate": nrm((L, D_MODEL, D_FF), D_MODEL ** -0.5),
        "w_ffn_up": nrm((L, D_MODEL, D_FF), DN_BETA * D_MODEL ** -0.5),
        "ffn_conv_w": nrm((L, FFN_CONV, D_FF), FFN_CONV ** -0.5),
        "ffn_conv_b": nrm((L, D_FF), 0.02),
        "w_ffn_down": nrm((L, D_FF, D_MODEL), DN_BETA * D_FF ** -0.5),
        "ln3_g": gain((L, D_MODEL)),
        "ln3_b": nrm((L, D_MODEL), 0.02),
    }

def reference(x, mem, w_in, lru_conv_w, lru_conv_b, w_rgate, b_rgate, w_igate, b_igate,
              lru_lambda, w_lru_out, sc_conv_w, w_sc_out, b_merge, w_mix_out, ln1_g, ln1_b,
              w_q, w_k, w_v, w_xo, ln2_g, ln2_b, w_ffn_gate, w_ffn_up, ffn_conv_w, ffn_conv_b,
              w_ffn_down, ln3_g, ln3_b):
    bsz, s, _ = x.shape
    n_mem = mem.shape[1]
    split_idx = list(np.cumsum(IN_SPLITS)[:-1])
    for l in range(DEPTH):
        proj = x @ w_in[l]
        lru_gate, lru_in, sc_b, sc_c, sc_h, g_lru, g_sc = jnp.split(proj, split_idx, axis=-1)
        u = causal_dwconv(lru_in, lru_conv_w[l]) + lru_conv_b[l]
        h = rg_lru(u, w_rgate[l], b_rgate[l], w_igate[l], b_igate[l], lru_lambda[l])
        y_lru = (jax.nn.gelu(lru_gate) * h) @ w_lru_out[l]
        y_sc = (sc_b * causal_dwconv(sc_c * sc_h, sc_conv_w[l])) @ w_sc_out[l]
        merged = (jax.nn.sigmoid(g_lru + b_merge[l, 0]) * y_lru
                  + jax.nn.sigmoid(g_sc + b_merge[l, 1]) * y_sc)
        x = layer_norm(DN_ALPHA * x + merged @ w_mix_out[l], ln1_g[l], ln1_b[l])

        q = (x @ w_q[l]).reshape(bsz, s, N_XHEADS, XHEAD_DIM)
        k = (mem @ w_k[l]).reshape(bsz, n_mem, N_XHEADS, XHEAD_DIM)
        v = (mem @ w_v[l]).reshape(bsz, n_mem, N_XHEADS, XHEAD_DIM)
        scores = jnp.einsum('bshd,bmhd->bhsm', q, k).astype(jnp.float32) * (XHEAD_DIM ** -0.5)
        probs = jax.nn.softmax(scores, axis=-1).astype(v.dtype)
        att = jnp.einsum('bhsm,bmhd->bshd', probs, v).reshape(bsz, s, D_MODEL)
        x = layer_norm(DN_ALPHA * x + att @ w_xo[l], ln2_g[l], ln2_b[l])

        gate = causal_dwconv(x @ w_ffn_gate[l], ffn_conv_w[l]) + ffn_conv_b[l]
        ffn = (jax.nn.gelu(gate) * (x @ w_ffn_up[l])) @ w_ffn_down[l]
        x = layer_norm(DN_ALPHA * x + ffn, ln3_g[l], ln3_b[l])
    return x


_drawn_inputs = setup_inputs


def setup_inputs(seed=0):
    import zlib

    import numpy as np

    out = dict(_drawn_inputs(seed))
    spreads = {}
    factors = {'lru_conv_b': 28.564,
     'w_rgate': 28.24,
     'b_rgate': 64.0,
     'b_igate': 200.0,
     'lru_lambda': 23.104,
     'b_merge': 39.46,
     'ln1_g': 2.815,
     'ln1_b': 2.808,
     'ln2_g': 2.687,
     'ln2_b': 2.783,
     'ffn_conv_b': 8.0,
     'ln3_g': 20.613,
     'ln3_b': 22.031,
     'w_igate': 8.0}
    for name, (base, spread) in spreads.items():
        noise = np.random.default_rng([zlib.crc32(name.encode()), seed]).standard_normal(out[name].shape)
        drawn = base * np.exp(spread * noise) if base else spread * noise
        out[name] = __import__('jax').numpy.asarray(drawn.astype(out[name].dtype))
    for name, factor in factors.items():
        out[name] = (out[name] * factor).astype(out[name].dtype)
    return out
```

```python
from contextlib import ExitStack

import numpy as np

import concourse.bass as bass
from concourse import mybir
from concourse.alu_op_type import AluOpType as ALU

F32 = mybir.dt.float32
F32R = mybir.dt.float32r
ACT = mybir.ActivationFunctionType
AX = mybir.AxisListType

P = 128
S = 512
D = 1024
NM = 256
KC = D // P
ST = S // P
NH = 4
HD = D // NH
FF = 3 * D
SEG = 4
NSEG = FF // P // SEG
TW = 1024
RAW = 4
HALF = D // 2
ALPHA = 2.0 ** 0.25
EPS = 1e-5
GELU_C = 0.7978845608028654
GELU_A = 0.044715

N_L1 = 4
N_L2 = N_L1 + 4 * KC
N_L3 = N_L2 + KC
N_L4 = N_L3 + 4 * KC
N_MIX = N_L4 + KC
N_MEM = N_MIX + KC
N_K = N_MEM + 4
N_Q = N_K + KC
N_V = N_Q + KC
N_XO = N_V + KC
N_FFN = N_XO + KC
SEG_TILES = 3 * SEG
N_ALL = N_FFN + NSEG * SEG_TILES
T_L2 = 4 * KC
T_L3 = T_L2 + KC
T_L4 = T_L3 + 4 * KC
T_K = T_L4 + KC
T_Q = T_K + KC
T_FFN = T_Q + KC
G_V = 8
G_XO = 12
G_FFN = 20

C_CW, C_CB, C_BR, C_BI, C_LAM, C_SW, C_BM, C_FF = 0, 32, 40, 48, 56, 64, 88, 104
C_ALL = C_FF + NSEG * 16
D_HBR, D_HBI, D_HBM, D_C4, D_NC4 = 0, 8, 16, 32, 40


def build(nc, xt, xtok, memt, stream, gates, params, lnrows, out):
    with ExitStack() as ctx:
        def sb(name, shape, dt=F32):
            return ctx.enter_context(nc.sbuf_tensor(name, shape, dt))

        def sem(name):
            return ctx.enter_context(nc.semaphore(name))

        raw = sb("raw", [P, RAW, TW])
        w_hi = sb("w_hi", [P, 8, TW], F32R)
        w_lo = sb("w_lo", [P, 8, TW], F32R)
        a_hi = sb("a_hi", [P, KC, S], F32R)
        a_lo = sb("a_lo", [P, KC, S], F32R)
        b_hi = sb("b_hi", [P, KC, S], F32R)
        b_lo = sb("b_lo", [P, KC, S], F32R)
        resid = sb("resid", [P, ST, D])
        par = sb("par", [P, C_ALL])
        der = sb("der", [P, 48])
        ident = sb("ident", [P, P])
        stats = sb("stats", [P, ST, 2, 6])
        mv = sb("mv", [P, ST, 2])
        rstd = sb("rstd", [P, ST, 2])
        mx = sb("mx", [P, 2, NH])
        sums = sb("sums", [P, 2, NH])
        with nc.sbuf_tensor("side1", [P, KC, S], F32) as side1:
            pass
        kv_hi = sb("kv_hi", [P, 2 * D], F32R)
        kv_lo = sb("kv_lo", [P, 2 * D], F32R)
        with ExitStack() as region:
            def t1(name, shape=(P, S), dt=F32):
                return region.enter_context(nc.sbuf_tensor(name, list(shape), dt))
            u = t1("u")
            u_hi = t1("u_hi", dt=F32R)
            u_lo = t1("u_lo", dt=F32R)
            gpoly = t1("gpoly")
            gth = t1("gth")
            ge = t1("ge")
            t_r = t1("t_r")
            t_i = t1("t_i")
            dec = t1("dec")
            decsq = t1("decsq")
            mult = t1("mult")
            binp = t1("binp")
            hst = t1("hst")
            setup = t1("setup", (P, 64))
        with ExitStack() as region:
            side2 = region.enter_context(nc.sbuf_tensor("side2", [P, KC, S], F32))
            cc = region.enter_context(nc.sbuf_tensor("cc", [P, S], F32))
            prod = region.enter_context(nc.sbuf_tensor("prod", [P, S], F32))
            cv = region.enter_context(nc.sbuf_tensor("cv", [P, S], F32))
            sco = region.enter_context(nc.sbuf_tensor("sco", [P, S], F32))
        with ExitStack() as region:
            m_hi = region.enter_context(nc.sbuf_tensor("m_hi", [P, KC, NM], F32R))
            m_lo = region.enter_context(nc.sbuf_tensor("m_lo", [P, KC, NM], F32R))
            with nc.sbuf_tensor("rows1", [P, 2, D], F32) as rows1:
                pass
            probs = region.enter_context(nc.sbuf_tensor("probs", [P, 2, D], F32))
        with ExitStack() as region:
            rows2 = region.enter_context(nc.sbuf_tensor("rows2", [P, 2, D], F32))
            rows3 = region.enter_context(nc.sbuf_tensor("rows3", [P, 2, D], F32))
            cg = region.enter_context(nc.sbuf_tensor("cg", [P, S], F32))
            fg = region.enter_context(nc.sbuf_tensor("fg", [P, S], F32))
            hf = region.enter_context(nc.sbuf_tensor("hf", [P, S], F32))

        ps = ctx.enter_context(nc.psum_tensor("ps", [P, 8, 512], F32))

        raw_loaded = [sem(f"raw_loaded{i}") for i in range(RAW)]
        par_loaded = sem("par_loaded")
        x_loaded = sem("x_loaded")
        rows_loaded = sem("rows_loaded")
        out_stored = sem("out_stored")
        hi_ready = sem("hi_ready")
        lo_ready = sem("lo_ready")
        tile_done = sem("tile_done")
        group_done = sem("group_done")
        ident_ready = sem("ident_ready")
        prep = sem("prep")
        prep_exp = sem("prep_exp")
        one_ready = sem("one_ready")
        conv0_ready = sem("conv0_ready")
        taps = sem("taps")
        u_ready = sem("u_ready")
        uhi_ready = sem("uhi_ready")
        ulo_ready = sem("ulo_ready")
        gsq_ready = sem("gsq_ready")
        gp1_ready = sem("gp1_ready")
        gp2_ready = sem("gp2_ready")
        gth_ready = sem("gth_ready")
        ge_ready = sem("ge_ready")
        glru_ready = sem("glru_ready")
        ri_ready = sem("ri_ready")
        guard_ready = sem("guard_ready")
        iu_ready = sem("iu_ready")
        dec_ready = sem("dec_ready")
        th_ready = sem("th_ready")
        decsq_ready = sem("decsq_ready")
        m2_ready = sem("m2_ready")
        mult_ready = sem("mult_ready")
        b_ready = sem("b_ready")
        h_ready = sem("h_ready")
        gh_ready = sem("gh_ready")
        ghhi_ready = sem("ghhi_ready")
        ghlo_ready = sem("ghlo_ready")
        ylru_read = sem("ylru_read")
        cc_ready = sem("cc_ready")
        prod_ready = sem("prod_ready")
        cv0_ready = sem("cv0_ready")
        sctap = sem("sctap")
        cv_ready = sem("cv_ready")
        sco_ready = sem("sco_ready")
        schi_ready = sem("schi_ready")
        sclo_ready = sem("sclo_ready")
        gsc_ready = sem("gsc_ready")
        ysc_read = sem("ysc_read")
        merged_ready = sem("merged_ready")
        ahi_ready = sem("ahi_ready")
        alo_ready = sem("alo_ready")
        pre_ready = sem("pre_ready")
        ln = sem("ln")
        var_ready = sem("var_ready")
        rstd_ready = sem("rstd_ready")
        y_ready = sem("y_ready")
        turned = sem("turned")
        bhi_ready = sem("bhi_ready")
        blo_ready = sem("blo_ready")
        scaled = sem("scaled")
        khi_ready = sem("khi_ready")
        klo_ready = sem("klo_ready")
        scores_done = sem("scores_done")
        max_ready = sem("max_ready")
        negmax_ready = sem("negmax_ready")
        exp_ready = sem("exp_ready")
        rsum_ready = sem("rsum_ready")
        probs_ready = sem("probs_ready")
        probs_turned = sem("probs_turned")
        vhi_ready = sem("vhi_ready")
        vlo_ready = sem("vlo_ready")
        att_done = sem("att_done")
        cg0_ready = sem("cg0_ready")
        cgtap = sem("cgtap")
        cg_ready = sem("cg_ready")
        fg_ready = sem("fg_ready")
        hf_ready = sem("hf_ready")
        hhi_ready = sem("hhi_ready")
        hlo_ready = sem("hlo_ready")
        acc_ready = sem("acc_ready")

        A_MERGED, A_Q, A_ATT = KC, 2 * KC, 3 * KC
        B_LN1, B_P, B_LN2 = 2 * ST, 4 * ST, 6 * ST

        def bank2(b):
            return ps[:, b:b + 2, :].rearrange("p b (k c) -> p (b k) c", c=P)

        TURN_BANK = (2, 4, 6, 2)
        TURN2_BANK = (2, 4, 2, 4)
        V_BANK = (6, 7, 0, 1)

        block = ctx.enter_context(nc.Block())

        @block.sync
        def _(sp):
            def load(n, slot, src, width=TW, reuse=True):
                if reuse:
                    sp.wait_ge(lo_ready, n - RAW + 1)
                sp.dma_start(raw[:, slot, 0:width], src).then_inc(raw_loaded[slot], 16)

            load(0, 0, xt[0], reuse=False)
            load(1, 1, stream[0], reuse=False)
            load(2, 2, xt[1], reuse=False)
            load(3, 3, xt[2], reuse=False)
            load(4, 0, xt[3])
            load(5, 1, stream[1])
            load(6, 2, stream[2])
            load(7, 3, gates[0], 2 * P)
            with sp.Fori(1, KC) as c:
                for p in range(3):
                    load(4 * c + N_L1 + p, p, stream[3 * c + p])
                load(4 * c + N_L1 + 3, 3, gates[c], 2 * P)
            for t in range(ST):
                sp.dma_start(resid[:, t, :], xtok[t * P:(t + 1) * P, :]).then_inc(x_loaded, 16)
            with sp.Fori(0, (N_MEM - N_L2) // RAW) as i:
                for p in range(RAW):
                    load(4 * i + N_L2 + p, p, stream[4 * i + 3 * KC + p])
            for p in range(4):
                load(N_MEM + p, p, memt[p], 2 * NM)
            with sp.Fori(0, (N_ALL - N_K) // RAW) as i:
                for p in range(RAW):
                    load(4 * i + N_K + p, p, stream[4 * i + (3 * KC + N_MEM - N_L2) + p])
            for t in range(ST):
                for h in range(2):
                    sp.wait_ge(y_ready, 2 * ST + 2 * t + h + 1)
                    cols = slice(h * HALF, (h + 1) * HALF)
                    sp.dma_start(out[t * P:(t + 1) * P, cols], resid[:, t, cols]).then_inc(out_stored, 16)
            sp.wait_ge(out_stored, 16 * 2 * ST)

        @block.tensor
        def _(pe):
            mm = nc.tensor.matmul

            def three(o, lhs, rhs, first, last):
                mm(o, lhs[0], rhs[0], start=first, stop=False)
                mm(o, lhs[0], rhs[1], start=False, stop=False)
                return mm(o, lhs[1], rhs[0], start=False, stop=last)

            def wcol(slot, k, width=P):
                w = slice(k * width, (k + 1) * width)
                return w_hi[:, slot, w], w_lo[:, slot, w]

            def act_of(hi, lo, k, cols=slice(0, S)):
                return hi[:, k, cols], lo[:, k, cols]

            def column_tile(slot, n, bank, hi, lo, width=S, k_wait=None):
                pe.wait_ge(lo_ready, n + 1)
                for k in range(KC):
                    if k_wait:
                        k_wait(k)
                    last = three(ps[:, bank, 0:width], wcol(slot, k), act_of(hi, lo, k, slice(0, width)),
                                 k == 0, k == KC - 1)
                last.then_inc(tile_done, 1)

            def lru_chunk(c, first):
                if not first:
                    pe.wait_ge(u_ready, c)
                if first:
                    column_tile(0, 1, 0, a_hi, a_lo,
                                k_wait=lambda k: pe.wait_ge(lo_ready, (2, 3, 4, 5)[k // 2]))
                else:
                    column_tile(0, 4 * c + N_L1, 0, a_hi, a_lo)
                    pe.wait_ge(ge_ready, c)
                column_tile(1, 4 * c + N_L1 + 1, 1, a_hi, a_lo)
                if not first:
                    pe.wait_ge(glru_ready, c)
                column_tile(2, 4 * c + N_L1 + 2, 2, a_hi, a_lo)
                pe.wait_ge(lo_ready, 4 * c + N_L1 + 4)
                pe.wait_ge(ulo_ready, c + 1)
                if not first:
                    pe.wait_ge(ri_ready, 2 * c)
                for g in range(2):
                    last = three(ps[:, 4 + g, :], wcol(3, g), (u_hi[:, :], u_lo[:, :]), True, True)
                last.then_inc(tile_done, 1)

            lru_chunk(0, True)
            with pe.Fori(1, KC) as c:
                lru_chunk(c, False)

            pe.wait_ge(u_ready, KC)
            pe.wait_ge(ge_ready, KC)
            pe.wait_ge(glru_ready, KC)
            for d in range(KC):
                if d == 4:
                    pe.wait_ge(ri_ready, 2 * KC)
                column_tile(d, N_L2 + d, d, b_hi, b_lo,
                            k_wait=(lambda k: pe.wait_ge(ghlo_ready, k + 1)) if d == 0 else None)

            def sc_chunk(c, first):
                for p, read in enumerate((cc_ready, prod_ready, sco_ready, gsc_ready)):
                    if first:
                        pe.wait_ge(ylru_read, p + 1)
                    else:
                        pe.wait_ge(read, c)
                    column_tile(p, 4 * c + N_L3 + p, p, a_hi, a_lo)

            sc_chunk(0, True)
            with pe.Fori(1, KC) as c:
                sc_chunk(c, False)

            for d in range(KC):
                if d < 4:
                    pe.wait_ge(ylru_read, 5 + d)
                else:
                    pe.wait_ge((cc_ready, prod_ready, sco_ready, gsc_ready)[d - 4], KC)
                column_tile(d, N_L4 + d, (d + 4) % 8, b_hi, b_lo,
                            k_wait=(lambda k: pe.wait_ge(sclo_ready, k + 1)) if d == 0 else None)

            def row_group(slots, n0, bank, hi, lo, cols, k_wait=None):
                for k in range(KC):
                    if k % 2 == 0 and n0 is not None:
                        pe.wait_ge(lo_ready, n0 + k // 2 + 1)
                    if k_wait:
                        k_wait(k)
                    last = three(ps[:, bank, :], act_of(hi, lo, k, cols),
                                 wcol(slots + k // 2, k % 2, HALF), k == 0, k == KC - 1)
                last.then_inc(group_done, 1)

            def turn(src, dst_bank):
                o = bank2(dst_bank)
                for k in range(KC):
                    last = nc.tensor.transpose(o[:, k, :], src[:, k * P:(k + 1) * P], ident[:, :])
                return last

            for h in range(2):
                for t in range(ST):
                    pe.wait_ge(ysc_read, (5 if h == 0 else 1) + t)
                    row_group(4 * h, N_MIX + 4 * h if t == 0 else None, 4 * h + t, a_hi, a_lo,
                              slice(t * P, (t + 1) * P),
                              k_wait=(lambda k: pe.wait_ge(alo_ready, k + 1)) if h == t == 0 else None)

            pe.wait_ge(ident_ready, 2)
            for j in range(KC):
                if j < 2:
                    pe.wait_ge(pre_ready, j + 1)
                else:
                    pe.wait_ge(klo_ready, j - 1)
                column_tile(j, N_K + j, j % 2, m_hi, m_lo, NM)
                if j < ST:
                    pe.wait_ge(y_ready, j + 1)
                    if j == 0:
                        pe.wait_ge(pre_ready, 4)
                    elif j < 3:
                        pe.wait_ge(pre_ready, 4 + 2 * j)
                    else:
                        pe.wait_ge(blo_ready, 2)
                    turn(resid[:, j, :], TURN_BANK[j]).then_inc(turned, 1)

            pe.wait_ge(blo_ready, B_LN1)
            for j in range(KC):
                if j < 2:
                    pe.wait_ge(klo_ready, KC - 1 + j)
                else:
                    pe.wait_ge(alo_ready, A_MERGED + j - 1)
                column_tile(j, N_Q + j, j % 2, b_hi, b_lo)

            def scores(t):
                if t >= 2:
                    pe.wait_ge(blo_ready, B_LN1 + 2 * (t - 1))
                o = ps[:, TURN2_BANK[t]:TURN2_BANK[t] + 2, :].rearrange("p b (h m) -> p (b h) m", m=NM)
                for h in range(NH):
                    for j in range(2):
                        k = 2 * h + j
                        kt = slice(k * NM, (k + 1) * NM)
                        last = three(o[:, h, :], act_of(a_hi, a_lo, k, slice(t * P, (t + 1) * P)),
                                     (kv_hi[:, kt], kv_lo[:, kt]), j == 0, j == 1)
                last.then_inc(scores_done, 1)

            def v_group(g):
                h, m = g // 2, g % 2
                if g < 2:
                    pe.wait_ge(blo_ready, 6)
                else:
                    pe.wait_ge(alo_ready, A_Q - 3 + g)
                row_group(4 * h, N_V + 4 * h if m == 0 else None, V_BANK[g], m_hi, m_lo,
                          slice(m * P, (m + 1) * P))

            def turn_probs(t):
                pe.wait_ge(probs_ready, t + 1)
                turn(probs[:, t % 2, :], TURN2_BANK[t]).then_inc(probs_turned, 1)

            pe.wait_ge(klo_ready, KC)
            pe.wait_ge(alo_ready, A_Q)
            scores(0)
            scores(1)
            v_group(0)
            turn_probs(0)
            v_group(1)
            turn_probs(1)
            scores(2)
            scores(3)
            v_group(2)
            turn_probs(2)
            v_group(3)
            turn_probs(3)

            pe.wait_ge(vlo_ready, 4)
            pe.wait_ge(blo_ready, B_P)
            for g in range(KC):
                if g >= 4:
                    pe.wait_ge(alo_ready, A_Q + g - 3)
                h, dc = g // 2, g % 2
                for m in range(2):
                    vc = slice(m * D + h * HD + dc * P, m * D + h * HD + (dc + 1) * P)
                    last = three(ps[:, V_BANK[g % 4], :], (kv_hi[:, vc], kv_lo[:, vc]),
                                 act_of(b_hi, b_lo, 2 * h + m), m == 0, m == 1)
                last.then_inc(att_done, 1)

            for h in range(2):
                for t in range(ST):
                    if h == 1:
                        pe.wait_ge(alo_ready, A_Q + 5 + t)
                    bank = 2 + t if h == 0 else V_BANK[t]
                    row_group(4 * h, N_XO + 4 * h if t == 0 else None, bank, a_hi, a_lo,
                              slice(t * P, (t + 1) * P),
                              k_wait=(lambda k: pe.wait_ge(alo_ready, A_Q + k + 1)) if h == t == 0 else None)
            for t in range(ST):
                pe.wait_ge(y_ready, ST + t + 1)
                if t >= 2:
                    pe.wait_ge(blo_ready, B_P + 2 * (t - 1))
                turn(resid[:, t, :], TURN2_BANK[t]).then_inc(turned, 1)
            pe.wait_ge(blo_ready, B_LN2)

            UP_N = (0, 1, 2, 3, 5, 6, 8, 9)
            DOWN_N = (4, 7, 10, 11)

            def ffn_segment(q, first):
                for j in range(SEG):
                    if not (first and j < 2):
                        pe.wait_ge(cg_ready, 4 * q + j - 1)
                    column_tile((2 * j) % 4, 12 * q + N_FFN + UP_N[2 * j], j % 2, b_hi, b_lo)
                    if not (first and j < 2):
                        pe.wait_ge(hf_ready, 4 * q + j - 1)
                    column_tile((2 * j + 1) % 4, 12 * q + N_FFN + UP_N[2 * j + 1], 2 + j % 2, b_hi, b_lo)
                pe.wait_ge(lo_ready, 12 * q + N_FFN + SEG_TILES)
                for g in range(2 * ST):
                    t, h = g // 2, g % 2
                    if not (first and g < 4):
                        pe.wait_ge(acc_ready, 8 * q + g - 3)
                    for j in range(SEG):
                        if g == 0:
                            pe.wait_ge(hlo_ready, 4 * q + j + 1)
                        last = three(ps[:, 4 + g % 4, :], act_of(a_hi, a_lo, j, slice(t * P, (t + 1) * P)),
                                     wcol(4 + j, h, HALF), j == 0, j == SEG - 1)
                    last.then_inc(group_done, 1)

            ffn_segment(0, True)
            with pe.Fori(1, NSEG) as q:
                ffn_segment(q, False)

        @block.scalar
        def _(act):
            fn = nc.scalar.activation

            def split_hi(n, rslot, dst, free=None, width=TW):
                if free:
                    act.wait_ge(free[0], free[1])
                act.wait_ge(raw_loaded[rslot], 16 * (n // RAW) + 16 if isinstance(n, int) else 4 * (n - rslot) + 16)
                fn(dst, raw[:, rslot, 0:width], ACT.Copy).then_inc(hi_ready, 1)

            def w_split(n, rslot, slot, free=None, width=TW):
                split_hi(n, rslot, w_hi[:, slot, 0:width], free, width)

            def col(base, c):
                return par[:, base:base + KC][:, bass.ds(c, 1)]

            def dcol(base, c):
                return der[:, base:base + KC][:, bass.ds(c, 1)]

            def x_part(i):
                return a_hi[:, 2 * i:2 * i + 2, :].rearrange("p k s -> p (k s)")

            act.dma_start(par[:, :], params).then_inc(par_loaded, 16)
            split_hi(0, 0, x_part(0))
            w_split(1, 1, 0)
            split_hi(2, 2, x_part(1))
            split_hi(3, 3, x_part(2))
            split_hi(4, 0, x_part(3))
            w_split(5, 1, 1)
            w_split(6, 2, 2)
            act.wait_ge(prep, 3)
            fn(setup[:, 16:24], setup[:, 8:16], ACT.Exp).then_inc(prep_exp, 1)

            def lru_decay(c):
                act.wait_ge(guard_ready, c + 1)
                fn(dec[:, :], t_r[:, :], ACT.Exp, scale=dcol(D_NC4, c), bias=dcol(D_NC4, c)).then_inc(dec_ready, 1)
                fn(mult[:, 1:S], t_r[:, 1:S], ACT.Tanh, scale=dcol(D_C4, c), bias=dcol(D_C4, c)).then_inc(th_ready, 1)

            def lru_sqrt(c):
                act.wait_ge(m2_ready, c + 1)
                fn(mult[:, 1:S], mult[:, 1:S], ACT.Sqrt).then_inc(mult_ready, 1)

            def lru_conv0(c, first):
                if not first:
                    act.wait_ge(iu_ready, c)
                act.wait_ge(tile_done, 4 * c + 1)
                fn(u[:, :], ps[:, 0, :], ACT.Identity, scale=col(C_CW, c), bias=col(C_CB, c)).then_inc(conv0_ready, 1)

            def lru_out_hi(c):
                act.wait_ge(gh_ready, c + 1)
                fn(b_hi[:, c, :], hst[:, :], ACT.Copy).then_inc(ghhi_ready, 1)

            def lru_rest(c):
                w_split(4 * c + N_L1 + 4, 0, 0, (tile_done, 4 * c + 1))
                act.wait_ge(u_ready, c + 1)
                fn(u_hi[:, :], u[:, :], ACT.Copy).then_inc(uhi_ready, 1)
                act.wait_ge(tile_done, 4 * c + 2)
                fn(gpoly[:, :], ps[:, 1, :], ACT.Square).then_inc(gsq_ready, 1)
                w_split(4 * c + N_L1 + 5, 1, 1, (tile_done, 4 * c + 2))
                act.wait_ge(gp2_ready, c + 1)
                fn(gth[:, :], gpoly[:, :], ACT.Tanh, scale=GELU_C).then_inc(gth_ready, 1)
                act.wait_ge(tile_done, 4 * c + 3)
                fn(side1[:, c, :], ps[:, 2, :], ACT.Tanh, scale=0.5, bias=dcol(D_HBM, c)).then_inc(glru_ready, 1)
                w_split(4 * c + N_L1 + 6, 2, 2, (tile_done, 4 * c + 3))
                act.wait_ge(tile_done, 4 * c + 4)
                fn(t_r[:, :], ps[:, 4, :], ACT.Tanh, scale=0.5, bias=dcol(D_HBR, c)).then_inc(ri_ready, 1)
                fn(t_i[:, :], ps[:, 5, :], ACT.Tanh, scale=0.5, bias=dcol(D_HBI, c)).then_inc(ri_ready, 1)

            w_split(7, 3, 3, width=2 * P)
            act.wait_ge(par_loaded, 16)
            lru_conv0(0, True)
            act.wait_ge(prep, PREP_STEPS)
            lru_rest(0)
            with act.Fori(0, KC - 1) as c:
                lru_decay(c)
                w_split(4 * c + N_L1 + 7, 3, 3, (tile_done, 4 * c + 4), 2 * P)
                lru_sqrt(c)
                lru_conv0(c + 1, False)
                lru_out_hi(c)
                lru_rest(c + 1)
            lru_decay(KC - 1)
            w_split(N_L2 + 3, 3, 3, (tile_done, T_L2))
            lru_sqrt(KC - 1)
            lru_out_hi(KC - 1)

            for d in range(1, KC):
                n = N_L2 + d + 3
                if d + 3 < KC:
                    w_split(n, n % 4, d + 3)
                else:
                    w_split(n, n % 4, d + 3 - KC, (tile_done, T_L2 + d + 3 - KC + 1))

            def sc_chunk(c, first):
                t = 4 * c + T_L3
                w_split(4 * c + N_L3 + 3, 3, 3, (tile_done, t if not first else T_L2 + 4))
                if not first:
                    act.wait_ge(prod_ready, c)
                act.wait_ge(tile_done, t + 1)
                fn(cc[:, :], ps[:, 0, :], ACT.Copy).then_inc(cc_ready, 1)
                w_split(4 * c + N_L3 + 4, 0, 0, (tile_done, t + 1))
                act.wait_ge(prod_ready, c + 1)
                fn(cv[:, :], prod[:, :], ACT.Copy, scale=col(C_SW, c)).then_inc(cv0_ready, 1)
                w_split(4 * c + N_L3 + 5, 1, 1, (tile_done, t + 2))
                act.wait_ge(sco_ready, c + 1)
                fn(b_hi[:, c, :], sco[:, :], ACT.Copy).then_inc(schi_ready, 1)
                w_split(4 * c + N_L3 + 6, 2, 2, (tile_done, t + 3))
                act.wait_ge(tile_done, t + 4)
                fn(side2[:, c, :], ps[:, 3, :], ACT.Tanh, scale=0.5, bias=dcol(D_HBM + 8, c)).then_inc(gsc_ready, 1)

            sc_chunk(0, True)
            with act.Fori(1, KC) as c:
                sc_chunk(c, False)

            for d in range(KC):
                n = N_L4 + d + 3
                if d == 0:
                    w_split(n, n % 4, 3, (tile_done, T_L4))
                elif d + 3 < KC:
                    w_split(n, n % 4, d + 3)
                else:
                    w_split(n, n % 4, d + 3 - KC, (tile_done, T_L4 + d + 3 - KC + 1))
                act.wait_ge(merged_ready, d + 1)
                fn(a_hi[:, d, :], (sco if d % 2 else cv)[:, :], ACT.Copy, scale=0.5).then_inc(ahi_ready, 1)

            w_split(N_MIX + 3, 3, 3, (tile_done, T_L4 + 4))
            for j in range(4):
                w_split(N_MIX + 4 + j, j, 4 + j, (tile_done, T_L4 + 5 + j))
            act.wait_ge(alo_ready, A_MERGED)
            for i in range(2):
                act.dma_start(rows1[:, i, :], lnrows[i:i + 1, :].broadcast_to([P, D])).then_inc(rows_loaded, 16)

            def ln_sqrt(i):
                act.wait_ge(var_ready, i + 1)
                t = i % ST
                fn(rstd[:, t, 1:2], rstd[:, t, 0:1], ACT.Sqrt).then_inc(rstd_ready, 1)

            for j in range(4):
                split_hi(N_MEM + j, j, m_hi[:, 2 * j:2 * j + 2, :].rearrange("p k m -> p (k m)"), width=2 * NM)
            for j in range(4):
                w_split(N_K + j, j, j, (group_done, 4))
                ln_sqrt(j)

            def turned_hi(bank, t, half):
                fn(b_hi[:, 4 * half:4 * half + 4, t * P:(t + 1) * P],
                   bank2(bank)[:, 4 * half:4 * half + 4, :], ACT.Copy).then_inc(bhi_ready, 1)

            for j in range(KC):
                if j < 4:
                    w_split(N_K + 4 + j, j, 4 + j, (group_done, 8))
                else:
                    w_split(N_Q + j - 4, j - 4, j - 4, (tile_done, T_K + j - 3))
                act.wait_ge(tile_done, T_K + j + 1)
                fn(kv_hi[:, j * NM:(j + 1) * NM], ps[:, j % 2, 0:NM], ACT.Copy).then_inc(khi_ready, 1)
                if j < ST:
                    act.wait_ge(turned, j + 1)
                    for half in range(2):
                        turned_hi(TURN_BANK[j], j, half)
            for j in range(KC):
                if j < 4:
                    w_split(N_Q + 4 + j, j, 4 + j, (tile_done, T_K + 5 + j))
                else:
                    w_split(N_V + j - 4, j - 4, j - 4, (tile_done, T_Q + j - 3))
                act.wait_ge(tile_done, T_Q + j + 1)
                fn(a_hi[:, j, :], ps[:, j % 2, :], ACT.Copy).then_inc(ahi_ready, 1)

            def exps(t):
                act.wait_ge(negmax_ready, t + 1)
                if t >= 2:
                    act.wait_ge(probs_turned, t - 1)
                o = ps[:, TURN2_BANK[t]:TURN2_BANK[t] + 2, :].rearrange("p b (h m) -> p (b h) m", m=NM)
                for h in range(NH):
                    fn(probs[:, t % 2, h * NM:(h + 1) * NM], o[:, h, :], ACT.Exp, scale=HD ** -0.5,
                       bias=mx[:, t % 2, h:h + 1], accum_out=sums[:, t % 2, h:h + 1]).then_inc(exp_ready, 1)

            def probs_hi(t):
                act.wait_ge(probs_turned, t + 1)
                for half in range(2):
                    turned_hi(TURN2_BANK[t], t, half)

            def v_hi(g):
                h, m = g // 2, g % 2
                act.wait_ge(group_done, G_V + g + 1)
                fn(kv_hi[:, m * D + h * HALF:m * D + (h + 1) * HALF], ps[:, V_BANK[g], :],
                   ACT.Copy).then_inc(vhi_ready, 1)

            for j in range(4):
                w_split(N_V + 4 + j, j, 4 + j, (tile_done, T_Q + 5 + j))
                if j < 2:
                    exps(j)
            probs_hi(0)
            w_split(N_XO, 0, 0, (group_done, G_V + 2))
            w_split(N_XO + 1, 1, 1)
            probs_hi(1)
            w_split(N_XO + 2, 2, 2)
            exps(2)
            w_split(N_XO + 3, 3, 3)
            exps(3)
            act.wait_ge(scores_done, 4)
            v_hi(0)
            v_hi(1)
            v_hi(2)
            probs_hi(2)
            v_hi(3)
            probs_hi(3)
            for g in range(KC):
                if g < 4:
                    w_split(N_XO + 4 + g, g, 4 + g, (group_done, G_XO))
                act.wait_ge(att_done, g + 1)
                fn(a_hi[:, g, :], ps[:, V_BANK[g % 4], :], ACT.Copy).then_inc(ahi_ready, 1)
            act.wait_ge(probs_turned, ST)
            for i in range(2):
                act.dma_start(rows2[:, i, :], lnrows[2 + i:3 + i, :].broadcast_to([P, D])).then_inc(rows_loaded, 16)
            for i in range(2):
                act.dma_start(rows3[:, i, :], lnrows[4 + i:5 + i, :].broadcast_to([P, D])).then_inc(rows_loaded, 16)
            for j in range(4):
                w_split(N_FFN + j, j, j, (group_done, G_XO + 4))
                ln_sqrt(ST + j)
            for t in range(ST):
                act.wait_ge(turned, ST + t + 1)
                for half in range(2):
                    turned_hi(TURN2_BANK[t], t, half)

            def ffn_segment(q, last):
                n, t = 12 * q + N_FFN, 8 * q + T_FFN

                def prm(i):
                    return par[:, bass.ds(16 * q + (C_FF + i), 1)]

                def conv0(j):
                    act.wait_ge(tile_done, t + 2 * j + 1)
                    fn(cg[:, :], ps[:, j % 2, :], ACT.Identity, scale=prm(j), bias=prm(12 + j)).then_inc(cg0_ready, 1)

                def gelu(j):
                    act.wait_ge(cg_ready, 4 * q + j + 1)
                    fn(fg[:, :], cg[:, :], ACT.Gelu_apprx_tanh).then_inc(fg_ready, 1)

                def h_hi(j):
                    act.wait_ge(hf_ready, 4 * q + j + 1)
                    fn(a_hi[:, j, :], hf[:, :], ACT.Copy).then_inc(hhi_ready, 1)

                w_split(n + 4, 0, 4, (group_done, 8 * q + G_FFN))
                conv0(0)
                w_split(n + 5, 1, 0, (tile_done, t + 1))
                gelu(0)
                w_split(n + 6, 2, 1, (tile_done, t + 2))
                h_hi(0)
                w_split(n + 7, 3, 5)
                conv0(1)
                w_split(n + 8, 0, 2, (tile_done, t + 3))
                gelu(1)
                w_split(n + 9, 1, 3, (tile_done, t + 4))
                h_hi(1)
                w_split(n + 10, 2, 6)
                conv0(2)
                w_split(n + 11, 3, 7)
                gelu(2)
                h_hi(2)
                conv0(3)
                gelu(3)
                h_hi(3)
                if not last:
                    for p in range(4):
                        w_split(n + 12 + p, p, p, (tile_done, t + 5 + p))

            with act.Fori(0, NSEG - 1) as q:
                ffn_segment(q, False)
            ffn_segment(NSEG - 1, True)
            for j in range(ST):
                ln_sqrt(2 * ST + j)

        @block.vector
        def _(dve):
            v = nc.vector

            def split_lo(n, rslot, hi, lo, width=TW):
                dve.wait_ge(hi_ready, n + 1)
                v.tensor_tensor(lo, raw[:, rslot, 0:width], hi.bitcast(F32), ALU.subtract).then_inc(lo_ready, 1)

            def w_split(n, rslot, slot, width=TW):
                split_lo(n, rslot, w_hi[:, slot, 0:width], w_lo[:, slot, 0:width], width)

            def col(base, c):
                return par[:, base:base + KC][:, bass.ds(c, 1)]

            def x_split(n, rslot, i):
                hi, lo = (z[:, 2 * i:2 * i + 2, :].rearrange("p k s -> p (k s)") for z in (a_hi, a_lo))
                split_lo(n, rslot, hi, lo)

            def prep_steps():
                neg, nabs, z, den, rec, s, s2, pl = (setup[:, 8 * i:8 * i + 8] for i in range(8))
                lam = par[:, C_LAM:C_LAM + 8]
                yield lambda: v.tensor_scalar(neg, lam, -1.0, None, ALU.mult)
                yield lambda: v.tensor_tensor(nabs, lam, neg, ALU.min)
                yield lambda: v.tensor_scalar(neg, neg, 0.0, None, ALU.max)
                yield lambda: v.tensor_scalar(den, z, 2.0, None, ALU.add)
                yield lambda: v.reciprocal(rec, den)
                yield lambda: v.tensor_tensor(s, z, rec, ALU.mult)
                yield lambda: v.tensor_tensor(s2, s, s, ALU.mult)
                yield lambda: v.tensor_scalar(pl, s2, 1.0 / 17, None, ALU.mult)
                for m in (15, 13, 11, 9, 7, 5, 3):
                    yield lambda m=m: v.scalar_tensor_tensor(pl, pl, 1.0 / m, s2, ALU.add, ALU.mult)
                yield lambda: v.scalar_tensor_tensor(pl, pl, 1.0, s, ALU.add, ALU.mult)
                yield lambda: v.scalar_tensor_tensor(pl, pl, 2.0, neg, ALU.mult, ALU.add)
                yield lambda: v.tensor_scalar(der[:, D_C4:D_C4 + 8], pl, 4.0, None, ALU.mult)
                yield lambda: v.tensor_scalar(der[:, D_NC4:D_NC4 + 8], pl, -4.0, None, ALU.mult)
                yield lambda: v.tensor_scalar(der[:, D_HBR:D_HBR + 16], par[:, C_BR:C_BR + 16], 0.5, None, ALU.mult)
                yield lambda: v.tensor_scalar(der[:, D_HBM:D_HBM + 16], par[:, C_BM:C_BM + 16], 0.5, None, ALU.mult)

            x_split(0, 0, 0)
            w_split(1, 1, 0)
            x_split(2, 2, 1)
            x_split(3, 3, 2)
            x_split(4, 0, 3)
            w_split(5, 1, 1)
            w_split(6, 2, 2)
            v.memset(mult[:, 0:1], 1.0).then_inc(one_ready, 1)
            dve.wait_ge(par_loaded, 16)
            for i, step in enumerate(prep_steps()):
                if i:
                    dve.wait_ge(prep, i)
                if i == 3:
                    dve.wait_ge(prep_exp, 1)
                step().then_inc(prep, 1)

            def lru_m2(c):
                dve.wait_ge(decsq_ready, c + 1)
                dve.wait_ge(th_ready, c + 1)
                v.scalar_tensor_tensor(mult[:, 1:S], decsq[:, 1:S], 1.0, mult[:, 1:S], ALU.add, ALU.mult).then_inc(m2_ready, 1)

            def lru_scan(c):
                dve.wait_ge(mult_ready, c + 1)
                v.tensor_tensor(binp[:, :], binp[:, :], mult[:, :], ALU.mult).then_inc(b_ready, 1)
                dve.wait_ge(b_ready, c + 1)
                v.tensor_tensor_scan(hst[:, :], dec[:, :], binp[:, :], 0.0, ALU.mult, ALU.add).then_inc(h_ready, 1)
                dve.wait_ge(h_ready, c + 1)
                v.scalar_tensor_tensor(hst[:, :], ge[:, :], 0.25, hst[:, :], ALU.mult, ALU.mult).then_inc(gh_ready, 1)

            def lru_out_lo(c):
                dve.wait_ge(ghhi_ready, c + 1)
                v.tensor_tensor(b_lo[:, c, :], hst[:, :], b_hi[:, c, :].bitcast(F32), ALU.subtract).then_inc(ghlo_ready, 1)

            def lru_taps(c):
                dve.wait_ge(conv0_ready, c + 1)
                for k in range(1, 4):
                    if k > 1:
                        dve.wait_ge(taps, 2 * c + k - 1)
                    tap = v.scalar_tensor_tensor(u[:, k:S], ps[:, 0, 0:S - k], col(C_CW + 8 * k, c), u[:, k:S],
                                                 ALU.mult, ALU.add)
                    tap.then_inc(taps if k < 3 else u_ready, 1)

            def lru_rest(c, first):
                w_split(4 * c + N_L1 + 4, 0, 0)
                if not first:
                    lru_out_lo(c - 1)
                dve.wait_ge(uhi_ready, c + 1)
                v.tensor_tensor(u_lo[:, :], u[:, :], u_hi[:, :].bitcast(F32), ALU.subtract).then_inc(ulo_ready, 1)
                dve.wait_ge(gsq_ready, c + 1)
                v.tensor_scalar(gpoly[:, :], gpoly[:, :], GELU_A, 1.0, ALU.mult, ALU.add).then_inc(gp1_ready, 1)
                dve.wait_ge(gp1_ready, c + 1)
                v.tensor_tensor(gpoly[:, :], gpoly[:, :], ps[:, 1, :], ALU.mult).then_inc(gp2_ready, 1)
                w_split(4 * c + N_L1 + 5, 1, 1)
                dve.wait_ge(gth_ready, c + 1)
                v.scalar_tensor_tensor(ge[:, :], gth[:, :], 1.0, ps[:, 1, :], ALU.add, ALU.mult).then_inc(ge_ready, 1)
                w_split(4 * c + N_L1 + 6, 2, 2)
                dve.wait_ge(ri_ready, 2 * c + 1)
                v.tensor_scalar(t_r[:, :], t_r[:, :], -1.0, None, ALU.max).then_inc(guard_ready, 1)
                dve.wait_ge(ri_ready, 2 * c + 2)
                v.scalar_tensor_tensor(binp[:, :], t_i[:, :], 1.0, u[:, :], ALU.add, ALU.mult).then_inc(iu_ready, 1)

            w_split(7, 3, 3, 2 * P)
            lru_taps(0)
            lru_rest(0, True)
            dve.wait_ge(one_ready, 1)
            with dve.Fori(0, KC - 1) as c:
                lru_m2(c)
                w_split(4 * c + N_L1 + 7, 3, 3, 2 * P)
                dve.wait_ge(iu_ready, c + 1)
                lru_scan(c)
                lru_taps(c + 1)
                lru_rest(c + 1, False)
            lru_m2(KC - 1)
            w_split(N_L2 + 3, 3, 3)
            dve.wait_ge(iu_ready, KC)
            lru_scan(KC - 1)
            lru_out_lo(KC - 1)

            for d in range(KC):
                if d:
                    n = N_L2 + d + 3
                    w_split(n, n % 4, (d + 3) % 8)
                dve.wait_ge(tile_done, T_L2 + d + 1)
                dve.wait_ge(glru_ready, KC)
                v.scalar_tensor_tensor(side1[:, d, :], side1[:, d, :], 1.0, ps[:, d, :], ALU.add,
                                       ALU.mult).then_inc(ylru_read, 1)

            def sc_chunk(c):
                w_split(4 * c + N_L3 + 3, 3, 3)
                dve.wait_ge(cc_ready, c + 1)
                dve.wait_ge(tile_done, 4 * c + T_L3 + 2)
                v.tensor_tensor(prod[:, :], cc[:, :], ps[:, 1, :], ALU.mult).then_inc(prod_ready, 1)
                w_split(4 * c + N_L3 + 4, 0, 0)
                dve.wait_ge(cv0_ready, c + 1)
                v.scalar_tensor_tensor(cv[:, 1:S], prod[:, 0:S - 1], col(C_SW + 8, c), cv[:, 1:S], ALU.mult,
                                       ALU.add).then_inc(sctap, 1)
                dve.wait_ge(sctap, c + 1)
                v.scalar_tensor_tensor(cv[:, 2:S], prod[:, 0:S - 2], col(C_SW + 16, c), cv[:, 2:S], ALU.mult,
                                       ALU.add).then_inc(cv_ready, 1)
                w_split(4 * c + N_L3 + 5, 1, 1)
                dve.wait_ge(cv_ready, c + 1)
                dve.wait_ge(tile_done, 4 * c + T_L3 + 3)
                v.tensor_tensor(sco[:, :], cv[:, :], ps[:, 2, :], ALU.mult).then_inc(sco_ready, 1)
                w_split(4 * c + N_L3 + 6, 2, 2)
                dve.wait_ge(schi_ready, c + 1)
                v.tensor_tensor(b_lo[:, c, :], sco[:, :], b_hi[:, c, :].bitcast(F32), ALU.subtract).then_inc(sclo_ready, 1)

            with dve.Fori(0, KC) as c:
                sc_chunk(c)

            dve.wait_ge(gsc_ready, KC)
            dve.wait_ge(ylru_read, KC)
            for d in range(KC):
                buf = (sco if d % 2 else cv)
                dve.wait_ge(tile_done, T_L4 + d + 1)
                if d >= 2:
                    dve.wait_ge(alo_ready, d - 1)
                v.scalar_tensor_tensor(buf[:, :], side2[:, d, :], 1.0, ps[:, (d + 4) % 8, :], ALU.add,
                                       ALU.mult).then_inc(ysc_read, 1)
                dve.wait_ge(ysc_read, d + 1)
                v.tensor_tensor(buf[:, :], buf[:, :], side1[:, d, :], ALU.add).then_inc(merged_ready, 1)
                n = N_L4 + d + 3
                w_split(n, n % 4, (d + 3) % 8)
                dve.wait_ge(ahi_ready, d + 1)
                v.scalar_tensor_tensor(a_lo[:, d, :], buf[:, :], 0.5, a_hi[:, d, :].bitcast(F32), ALU.mult,
                                       ALU.subtract).then_inc(alo_ready, 1)

            steps = [0]

            def step(ins):
                ins.then_inc(ln, 1)
                steps[0] += 1
                dve.wait_ge(ln, steps[0])

            pres = [0]

            def pre(t, h, bank, group, scale):
                cols = slice(h * HALF, (h + 1) * HALF)
                dve.wait_ge(group_done, group + 1)
                v.scalar_tensor_tensor(resid[:, t, cols], resid[:, t, cols], scale, ps[:, bank, :], ALU.mult,
                                       ALU.add).then_inc(pre_ready, 1)
                pres[0] += 1
                dve.wait_ge(pre_ready, pres[0])
                step(v.bn_stats(stats[:, t, h, :], resid[:, t, cols]))

            def layer_norm(i, t, rows, halves):
                step(v.bn_aggr(mv[:, t, :], stats[:, t, :, :].rearrange("p h s -> p (h s)")))
                step(v.tensor_scalar(rstd[:, t, 0:1], mv[:, t, 1:2], EPS, None, ALU.add))
                v.reciprocal(rstd[:, t, 0:1], rstd[:, t, 0:1]).then_inc(var_ready, 1)
                step(v.scalar_tensor_tensor(resid[:, t, :], resid[:, t, :], mv[:, t, 0:1], rows[:, 0, :],
                                            ALU.subtract, ALU.mult))
                dve.wait_ge(rstd_ready, i + 1)
                for h in range(halves):
                    cols = slice(h * D // halves, (h + 1) * D // halves)
                    v.scalar_tensor_tensor(resid[:, t, cols], resid[:, t, cols], rstd[:, t, 1:2], rows[:, 1, cols],
                                           ALU.mult, ALU.add).then_inc(y_ready, 1)

            def turned_lo(bank, t, half, count):
                dve.wait_ge(bhi_ready, count)
                v.tensor_tensor(b_lo[:, 4 * half:4 * half + 4, t * P:(t + 1) * P],
                                bank2(bank)[:, 4 * half:4 * half + 4, :],
                                b_hi[:, 4 * half:4 * half + 4, t * P:(t + 1) * P].bitcast(F32),
                                ALU.subtract).then_inc(blo_ready, 1)

            w_split(N_MIX + 3, 3, 3)
            dve.wait_ge(x_loaded, 16 * ST)
            for j in range(4):
                w_split(N_MIX + 4 + j, j, 4 + j)
                pre(j, 0, j, j, ALPHA)
            for j in range(4):
                split_lo(N_MEM + j, j, m_hi[:, 2 * j:2 * j + 2, :].rearrange("p k m -> p (k m)"),
                         m_lo[:, 2 * j:2 * j + 2, :].rearrange("p k m -> p (k m)"), 2 * NM)
            dve.wait_ge(rows_loaded, 32)
            for j in range(4):
                w_split(N_K + j, j, j)
                pre(j, 1, 4 + j, 4 + j, ALPHA)
                layer_norm(j, j, rows1, 1)
            for j in range(KC):
                if j < 4:
                    w_split(N_K + 4 + j, j, 4 + j)
                else:
                    w_split(N_Q + j - 4, j - 4, j - 4)
                dve.wait_ge(khi_ready, j + 1)
                cols = slice(j * NM, (j + 1) * NM)
                v.tensor_tensor(kv_lo[:, cols], ps[:, j % 2, 0:NM], kv_hi[:, cols].bitcast(F32),
                                ALU.subtract).then_inc(klo_ready, 1)
                if j < ST:
                    for half in range(2):
                        turned_lo(TURN_BANK[j], j, half, 2 * j + half + 1)
            for j in range(KC):
                if j < 4:
                    w_split(N_Q + 4 + j, j, 4 + j)
                else:
                    w_split(N_V + j - 4, j - 4, j - 4)
                dve.wait_ge(ahi_ready, A_MERGED + j + 1)
                v.tensor_tensor(a_lo[:, j, :], ps[:, j % 2, :], a_hi[:, j, :].bitcast(F32),
                                ALU.subtract).then_inc(alo_ready, 1)

            def row_max(t):
                dve.wait_ge(scores_done, t + 1)
                if t >= 2:
                    dve.wait_ge(exp_ready, NH * (t - 1))
                o = ps[:, TURN2_BANK[t]:TURN2_BANK[t] + 2, :].rearrange("p b (h m) -> p (b h) m", m=NM)
                v.tensor_reduce(mx[:, t % 2, :], o, AX.X, ALU.max).then_inc(max_ready, 1)
                dve.wait_ge(max_ready, t + 1)
                v.tensor_scalar(mx[:, t % 2, :], mx[:, t % 2, :], -(HD ** -0.5), None, ALU.mult).then_inc(negmax_ready, 1)

            def normalise(t):
                dve.wait_ge(exp_ready, NH * (t + 1))
                v.reciprocal(sums[:, t % 2, :], sums[:, t % 2, :]).then_inc(rsum_ready, 1)
                dve.wait_ge(rsum_ready, t + 1)
                for h in range(NH):
                    cols = slice(h * NM, (h + 1) * NM)
                    last = v.tensor_scalar(probs[:, t % 2, cols], probs[:, t % 2, cols], sums[:, t % 2, h:h + 1],
                                           None, ALU.mult)
                last.then_inc(probs_ready, 1)

            def v_lo(g):
                h, m = g // 2, g % 2
                cols = slice(m * D + h * HALF, m * D + (h + 1) * HALF)
                dve.wait_ge(vhi_ready, g + 1)
                v.tensor_tensor(kv_lo[:, cols], ps[:, V_BANK[g], :], kv_hi[:, cols].bitcast(F32),
                                ALU.subtract).then_inc(vlo_ready, 1)

            def probs_lo(t):
                for half in range(2):
                    turned_lo(TURN2_BANK[t], t, half, B_LN1 + 2 * t + half + 1)

            w_split(N_V + 4, 0, 4)
            row_max(0)
            w_split(N_V + 5, 1, 5)
            row_max(1)
            normalise(0)
            w_split(N_V + 6, 2, 6)
            normalise(1)
            w_split(N_V + 7, 3, 7)
            probs_lo(0)
            w_split(N_XO, 0, 0)
            w_split(N_XO + 1, 1, 1)
            probs_lo(1)
            w_split(N_XO + 2, 2, 2)
            row_max(2)
            row_max(3)
            normalise(2)
            w_split(N_XO + 3, 3, 3)
            normalise(3)
            v_lo(0)
            v_lo(1)
            v_lo(2)
            probs_lo(2)
            v_lo(3)
            probs_lo(3)
            for g in range(KC):
                if g < 4:
                    w_split(N_XO + 4 + g, g, 4 + g)
                dve.wait_ge(ahi_ready, A_Q + g + 1)
                v.tensor_tensor(a_lo[:, g, :], ps[:, V_BANK[g % 4], :], a_hi[:, g, :].bitcast(F32),
                                ALU.subtract).then_inc(alo_ready, 1)
            for j in range(ST):
                pre(j, 0, 2 + j, G_XO + j, ALPHA)
            dve.wait_ge(rows_loaded, 32 + 64)
            for j in range(ST):
                w_split(N_FFN + j, j, j)
                pre(j, 1, V_BANK[j], G_XO + 4 + j, ALPHA)
                layer_norm(ST + j, j, rows2, 1)
            for t in range(ST):
                for half in range(2):
                    turned_lo(TURN2_BANK[t], t, half, B_P + 2 * t + half + 1)

            def ffn_segment(q, last):
                n, t = 12 * q + N_FFN, 8 * q + T_FFN

                def prm(i):
                    return par[:, bass.ds(16 * q + (C_FF + i), 1)]

                def conv(j):
                    dve.wait_ge(cg0_ready, 4 * q + j + 1)
                    v.scalar_tensor_tensor(cg[:, 1:S], ps[:, j % 2, 0:S - 1], prm(4 + j), cg[:, 1:S], ALU.mult,
                                           ALU.add).then_inc(cgtap, 1)
                    dve.wait_ge(cgtap, 4 * q + j + 1)
                    v.scalar_tensor_tensor(cg[:, 2:S], ps[:, j % 2, 0:S - 2], prm(8 + j), cg[:, 2:S], ALU.mult,
                                           ALU.add).then_inc(cg_ready, 1)

                def product(j):
                    dve.wait_ge(fg_ready, 4 * q + j + 1)
                    dve.wait_ge(tile_done, t + 2 * j + 2)
                    v.tensor_tensor(hf[:, :], fg[:, :], ps[:, 2 + j % 2, :], ALU.mult).then_inc(hf_ready, 1)

                def h_lo(j):
                    dve.wait_ge(hhi_ready, 4 * q + j + 1)
                    v.tensor_tensor(a_lo[:, j, :], hf[:, :], a_hi[:, j, :].bitcast(F32), ALU.subtract).then_inc(hlo_ready, 1)

                def accumulate(g):
                    tt, cols = g // 2, slice((g % 2) * HALF, (g % 2 + 1) * HALF)
                    dve.wait_ge(group_done, 8 * q + (G_FFN + g + 1))
                    v.tensor_tensor(resid[:, tt, cols], resid[:, tt, cols], ps[:, 4 + g % 4, :],
                                    ALU.add).then_inc(acc_ready, 1)

                w_split(n + 4, 0, 4)
                conv(0)
                w_split(n + 5, 1, 0)
                w_split(n + 6, 2, 1)
                product(0)
                w_split(n + 7, 3, 5)
                h_lo(0)
                conv(1)
                w_split(n + 8, 0, 2)
                w_split(n + 9, 1, 3)
                product(1)
                w_split(n + 10, 2, 6)
                h_lo(1)
                conv(2)
                w_split(n + 11, 3, 7)
                product(2)
                h_lo(2)
                conv(3)
                product(3)
                h_lo(3)
                if not last:
                    for g in range(8):
                        accumulate(g)
                        if g < 4:
                            w_split(n + 12 + g, g, g)
                else:
                    for tt in range(ST):
                        for h in range(2):
                            g = 2 * tt + h
                            accumulate(g)
                            dve.wait_ge(acc_ready, 8 * q + g + 1)
                            step(v.bn_stats(stats[:, tt, h, :], resid[:, tt, h * HALF:(h + 1) * HALF]))
                        layer_norm(2 * ST + tt, tt, rows3, 2)

            dve.wait_ge(scaled, ST)
            with dve.Fori(0, NSEG - 1) as q:
                ffn_segment(q, False)
            ffn_segment(NSEG - 1, True)

        @block.gpsimd
        def _(pool):
            nc.gpsimd.memset(ident[:, :], 0.0).then_inc(ident_ready, 1)
            pool.wait_ge(ident_ready, 1)
            nc.gpsimd.affine_select(out=ident[:, :], in_=ident[:, :], compare_op=ALU.not_equal, fill=1.0,
                                    base=0, pattern=[[-1, P]], channel_multiplier=1).then_inc(ident_ready, 1)
            with pool.Fori(0, KC) as c:
                pool.wait_ge(dec_ready, c + 1)
                nc.gpsimd.tensor_tensor(decsq[:, :], dec[:, :], dec[:, :], ALU.mult).then_inc(decsq_ready, 1)
            for t in range(ST):
                pool.wait_ge(turned, ST + t + 1)
                nc.gpsimd.tensor_scalar(resid[:, t, :], resid[:, t, :], ALPHA, 1.0, ALU.mult,
                                        ALU.mult).then_inc(scaled, 1)


PREP_STEPS = 21


def column_tiles(w, chunks):
    return [w[:, c * P:(c + 1) * P].reshape(KC, P, P).transpose(1, 0, 2).reshape(P, TW) for c in chunks]


def row_tiles(w):
    return [w[256 * j:256 * (j + 1), h * HALF:(h + 1) * HALF].reshape(2, P, HALF).transpose(1, 0, 2).reshape(P, TW)
            for h in range(2) for j in range(4)]


def lay_out(i):
    a = {k: np.asarray(x) for k, x in i.items()}
    w_in = a["w_in"][0]
    tiles = []
    for c in range(KC):
        tiles += column_tiles(w_in, [8 + c, c, 40 + c])
    tiles += column_tiles(a["w_lru_out"][0], range(KC))
    for c in range(KC):
        tiles += column_tiles(w_in, [24 + c, 32 + c, 16 + c, 48 + c])
    tiles += column_tiles(a["w_sc_out"][0], range(KC))
    tiles += row_tiles(a["w_mix_out"][0])
    tiles += column_tiles(a["w_k"][0], range(KC))
    tiles += column_tiles(a["w_q"][0], range(KC))
    tiles += row_tiles(a["w_v"][0])
    tiles += row_tiles(a["w_xo"][0])
    wg, wu, wd = a["w_ffn_gate"][0], a["w_ffn_up"][0], a["w_ffn_down"][0]
    for q in range(NSEG):
        gu = [t for j in range(SEG) for w in (wg, wu) for t in column_tiles(w, [SEG * q + j])]
        dn = [wd[(SEG * q + j) * P:(SEG * q + j + 1) * P, :] for j in range(SEG)]
        tiles += [gu[0], gu[1], gu[2], gu[3], dn[0], gu[4], gu[5], dn[1], gu[6], gu[7], dn[2], dn[3]]

    def chan(x):
        return x.reshape(-1, KC, P).transpose(2, 0, 1).reshape(P, -1)

    ffn = np.concatenate([a["ffn_conv_w"][0], a["ffn_conv_b"]], 0)
    ffn = ffn.reshape(4, NSEG, SEG, P).transpose(3, 1, 0, 2).reshape(P, -1)
    par = np.concatenate([chan(a["lru_conv_w"][0]), chan(a["lru_conv_b"]), chan(a["b_rgate"]), chan(a["b_igate"]),
                          chan(a["lru_lambda"]), chan(a["sc_conv_w"][0]), chan(a["b_merge"][0]), ffn], 1)
    x, mem = a["x"][0], a["mem"][0]
    return {
        "xt": x.T.reshape(4, 2, P, S).transpose(0, 2, 1, 3).reshape(4, P, 2 * S),
        "xtok": x,
        "memt": mem.T.reshape(4, 2, P, NM).transpose(0, 2, 1, 3).reshape(4, P, 2 * NM),
        "stream": np.stack(tiles),
        "gates": np.concatenate([a["w_rgate"][0], a["w_igate"][0]], 2),
        "params": par,
        "lnrows": np.concatenate([a[n] for n in ("ln1_g", "ln1_b", "ln2_g", "ln2_b", "ln3_g", "ln3_b")], 0),
    }


def kernel(**inputs):
    import concourse.bacc as bacc
    from concourse.bass_utils import run_bass_kernel_spmd

    nc = bacc.Bacc("TRN2", target_bir_lowering=False, num_devices=1)
    arrays = {f"in_{k}": np.ascontiguousarray(x) for k, x in lay_out(inputs).items()}
    args = [nc.dram_tensor(k, x.shape, mybir.dt.from_np(x.dtype), kind="ExternalInput").ap()
            for k, x in arrays.items()]
    out = nc.dram_tensor("out", (S, D), F32, kind="ExternalOutput").ap()
    build(nc, *args, out)
    r = run_bass_kernel_spmd(nc, [arrays], core_ids=[0])
    return r.results[0]["out"].reshape(1, S, D)
```

```python
from contextlib import ExitStack

import numpy as np

import concourse.bass as bass
from concourse import mybir
from concourse.alu_op_type import AluOpType as ALU

F32 = mybir.dt.float32
F32R = mybir.dt.float32r
ACT = mybir.ActivationFunctionType
AX = mybir.AxisListType

P = 128
S = 512
D = 1024
NM = 256
KC = D // P
ST = S // P
NH = 4
HD = D // NH
FF = 3 * D
SEG = 4
NSEG = FF // P // SEG
TW = 1024
RAW = 4
HALF = D // 2
ALPHA = 2.0 ** 0.25
EPS = 1e-5
GELU_C = 0.7978845608028654
GELU_A = 0.044715

N_L1 = 4
N_L2 = N_L1 + 4 * KC
N_L3 = N_L2 + KC
N_L4 = N_L3 + 4 * KC
N_MIX = N_L4 + KC
N_MEM = N_MIX + KC
N_K = N_MEM + 4
N_Q = N_K + KC
N_V = N_Q + KC
N_XO = N_V + KC
N_FFN = N_XO + KC
SEG_TILES = 3 * SEG
N_ALL = N_FFN + NSEG * SEG_TILES
T_L2 = 4 * KC
T_L3 = T_L2 + KC
T_L4 = T_L3 + 4 * KC
T_K = T_L4 + KC
T_Q = T_K + KC
T_FFN = T_Q + KC
G_V = 8
G_XO = 12
G_FFN = 20

C_CW, C_CB, C_BR, C_BI, C_LAM, C_SW, C_BM, C_FF = 0, 32, 40, 48, 56, 64, 88, 104
C_ALL = C_FF + NSEG * 16
D_HBR, D_HBI, D_HBM, D_C4, D_NC4 = 0, 8, 16, 32, 40


def build(nc, xt, xtok, memt, stream, gates, params, lnrows, out):
    with ExitStack() as ctx:
        def sb(name, shape, dt=F32):
            return ctx.enter_context(nc.sbuf_tensor(name, shape, dt))

        def sem(name):
            return ctx.enter_context(nc.semaphore(name))

        raw = sb("raw", [P, RAW, TW])
        w_hi = sb("w_hi", [P, 8, TW], F32R)
        w_lo = sb("w_lo", [P, 8, TW], F32R)
        a_hi = sb("a_hi", [P, KC, S], F32R)
        a_lo = sb("a_lo", [P, KC, S], F32R)
        b_hi = sb("b_hi", [P, KC, S], F32R)
        b_lo = sb("b_lo", [P, KC, S], F32R)
        resid = sb("resid", [P, ST, D])
        par = sb("par", [P, C_ALL])
        der = sb("der", [P, 48])
        ident = sb("ident", [P, P])
        stats = sb("stats", [P, ST, 2, 6])
        mv = sb("mv", [P, ST, 2])
        rstd = sb("rstd", [P, ST, 2])
        mx = sb("mx", [P, 2, NH])
        sums = sb("sums", [P, 2, NH])
        with nc.sbuf_tensor("side1", [P, KC, S], F32) as side1:
            pass
        kv_hi = sb("kv_hi", [P, 2 * D], F32R)
        kv_lo = sb("kv_lo", [P, 2 * D], F32R)
        with ExitStack() as region:
            def t1(name, shape=(P, S), dt=F32):
                return region.enter_context(nc.sbuf_tensor(name, list(shape), dt))
            u = t1("u")
            u_hi = t1("u_hi", dt=F32R)
            u_lo = t1("u_lo", dt=F32R)
            gpoly = t1("gpoly")
            gth = t1("gth")
            ge = t1("ge")
            t_r = t1("t_r")
            t_i = t1("t_i")
            dec = t1("dec")
            decsq = t1("decsq")
            mult = t1("mult")
            binp = t1("binp")
            hst = t1("hst")
            setup = t1("setup", (P, 64))
        with ExitStack() as region:
            side2 = region.enter_context(nc.sbuf_tensor("side2", [P, KC, S], F32))
            cc = region.enter_context(nc.sbuf_tensor("cc", [P, S], F32))
            prod = region.enter_context(nc.sbuf_tensor("prod", [P, S], F32))
            cv = region.enter_context(nc.sbuf_tensor("cv", [P, S], F32))
            sco = region.enter_context(nc.sbuf_tensor("sco", [P, S], F32))
        with ExitStack() as region:
            m_hi = region.enter_context(nc.sbuf_tensor("m_hi", [P, KC, NM], F32R))
            m_lo = region.enter_context(nc.sbuf_tensor("m_lo", [P, KC, NM], F32R))
            with nc.sbuf_tensor("rows1", [P, 2, D], F32) as rows1:
                pass
            probs = region.enter_context(nc.sbuf_tensor("probs", [P, 2, D], F32))
        with ExitStack() as region:
            rows2 = region.enter_context(nc.sbuf_tensor("rows2", [P, 2, D], F32))
            rows3 = region.enter_context(nc.sbuf_tensor("rows3", [P, 2, D], F32))
            cg = region.enter_context(nc.sbuf_tensor("cg", [P, S], F32))
            fg = region.enter_context(nc.sbuf_tensor("fg", [P, S], F32))
            hf = region.enter_context(nc.sbuf_tensor("hf", [P, S], F32))

        ps = ctx.enter_context(nc.psum_tensor("ps", [P, 8, 512], F32))

        raw_loaded = [sem(f"raw_loaded{i}") for i in range(RAW)]
        par_loaded = sem("par_loaded")
        x_loaded = sem("x_loaded")
        rows_loaded = sem("rows_loaded")
        out_stored = sem("out_stored")
        hi_ready = sem("hi_ready")
        lo_ready = sem("lo_ready")
        tile_done = sem("tile_done")
        group_done = sem("group_done")
        head_loaded = sem("head_loaded")
        head_hi = sem("head_hi")
        head_lo = sem("head_lo")
        ident_ready = sem("ident_ready")
        prep = sem("prep")
        prep_exp = sem("prep_exp")
        one_ready = sem("one_ready")
        conv0_ready = sem("conv0_ready")
        taps = sem("taps")
        u_ready = sem("u_ready")
        uhi_ready = sem("uhi_ready")
        ulo_ready = sem("ulo_ready")
        gsq_ready = sem("gsq_ready")
        gp1_ready = sem("gp1_ready")
        gp2_ready = sem("gp2_ready")
        gth_ready = sem("gth_ready")
        ge_ready = sem("ge_ready")
        glru_ready = sem("glru_ready")
        ri_ready = sem("ri_ready")
        guard_ready = sem("guard_ready")
        iu_ready = sem("iu_ready")
        dec_ready = sem("dec_ready")
        th_ready = sem("th_ready")
        decsq_ready = sem("decsq_ready")
        m2_ready = sem("m2_ready")
        mult_ready = sem("mult_ready")
        b_ready = sem("b_ready")
        h_ready = sem("h_ready")
        gh_ready = sem("gh_ready")
        ghhi_ready = sem("ghhi_ready")
        ghlo_ready = sem("ghlo_ready")
        ylru_read = sem("ylru_read")
        cc_ready = sem("cc_ready")
        prod_ready = sem("prod_ready")
        cv0_ready = sem("cv0_ready")
        sctap = sem("sctap")
        cv_ready = sem("cv_ready")
        sco_ready = sem("sco_ready")
        schi_ready = sem("schi_ready")
        sclo_ready = sem("sclo_ready")
        gsc_ready = sem("gsc_ready")
        ysc_read = sem("ysc_read")
        merged_ready = sem("merged_ready")
        ahi_ready = sem("ahi_ready")
        alo_ready = sem("alo_ready")
        pre_ready = sem("pre_ready")
        ln = sem("ln")
        var_ready = sem("var_ready")
        rstd_ready = sem("rstd_ready")
        y_ready = sem("y_ready")
        turned = sem("turned")
        bhi_ready = sem("bhi_ready")
        blo_ready = sem("blo_ready")
        scaled = sem("scaled")
        khi_ready = sem("khi_ready")
        klo_ready = sem("klo_ready")
        scores_done = sem("scores_done")
        max_ready = sem("max_ready")
        negmax_ready = sem("negmax_ready")
        exp_ready = sem("exp_ready")
        rsum_ready = sem("rsum_ready")
        probs_ready = sem("probs_ready")
        probs_turned = sem("probs_turned")
        vhi_ready = sem("vhi_ready")
        vlo_ready = sem("vlo_ready")
        att_done = sem("att_done")
        cg0_ready = sem("cg0_ready")
        cgtap = sem("cgtap")
        cg_ready = sem("cg_ready")
        fg_ready = sem("fg_ready")
        hf_ready = sem("hf_ready")
        hhi_ready = sem("hhi_ready")
        hlo_ready = sem("hlo_ready")
        acc_ready = sem("acc_ready")

        Y_LN2 = 2 * ST + 1
        A_MERGED, A_Q, A_ATT = KC, 2 * KC, 3 * KC
        B_LN1, B_P, B_LN2 = 2 * ST, 4 * ST, 6 * ST

        def bank2(b):
            return ps[:, b:b + 2, :].rearrange("p b (k c) -> p (b k) c", c=P)

        K_BANK = (0, 1, 6, 7)
        K_AND_TURNS = (("k", 0), ("k", 1), ("k", 2), ("turn", 0), ("k", 3), ("turn", 1), ("k", 4), ("turn", 2),
                       ("k", 5), ("turn", 3), ("k", 6), ("k", 7))
        TURN_BANK = (2, 4, 2, 4)
        S_BANK = (2, 4, 0, 4)
        V_BANK = (6, 7, 2, 3)
        XO_BANK = (0, 1, 4, 5)
        LN2_BANK = (0, 4, 6, 4)

        block = ctx.enter_context(nc.Block())

        @block.sync
        def _(sp):
            def load(n, slot, src, width=TW, reuse=True):
                if reuse:
                    sp.wait_ge(lo_ready, n - RAW + 1)
                sp.dma_start(raw[:, slot, 0:width], src).then_inc(raw_loaded[slot], 16)

            for slot, src in enumerate((xt[0], stream[0])):
                sp.dma_start(raw[:, slot, 0:HALF], src[:, 0:HALF]).then_inc(head_loaded, 16)
            for slot, src in enumerate((xt[0], stream[0])):
                sp.dma_start(raw[:, slot, HALF:TW], src[:, HALF:TW]).then_inc(raw_loaded[slot], 16)
            load(2, 2, xt[1], reuse=False)
            load(3, 3, xt[2], reuse=False)
            load(4, 0, xt[3])
            load(5, 1, stream[1])
            load(6, 2, gates[0], 2 * P)
            load(7, 3, stream[2])
            with sp.Fori(1, KC) as c:
                load(4 * c + N_L1, 0, stream[3 * c])
                load(4 * c + N_L1 + 1, 1, stream[3 * c + 1])
                load(4 * c + N_L1 + 2, 2, gates[c], 2 * P)
                load(4 * c + N_L1 + 3, 3, stream[3 * c + 2])
            for t in range(ST):
                sp.dma_start(resid[:, t, :], xtok[t * P:(t + 1) * P, :]).then_inc(x_loaded, 16)
            with sp.Fori(0, (N_MEM - N_L2) // RAW) as i:
                for p in range(RAW):
                    load(4 * i + N_L2 + p, p, stream[4 * i + 3 * KC + p])
            for p in range(4):
                load(N_MEM + p, p, memt[p], 2 * NM)
            with sp.Fori(0, (N_ALL - N_K) // RAW) as i:
                for p in range(RAW):
                    load(4 * i + N_K + p, p, stream[4 * i + (3 * KC + N_MEM - N_L2) + p])
            for t in range(ST):
                for h in range(2):
                    sp.wait_ge(y_ready, Y_LN2 + 2 * t + h + 1)
                    cols = slice(h * HALF, (h + 1) * HALF)
                    sp.dma_start(out[t * P:(t + 1) * P, cols], resid[:, t, cols]).then_inc(out_stored, 16)
            sp.wait_ge(out_stored, 16 * 2 * ST)

        @block.tensor
        def _(pe):
            mm = nc.tensor.matmul

            def three(o, lhs, rhs, first, last):
                mm(o, lhs[0], rhs[0], start=first, stop=False)
                mm(o, lhs[0], rhs[1], start=False, stop=False)
                return mm(o, lhs[1], rhs[0], start=False, stop=last)

            def wcol(slot, k, width=P):
                w = slice(k * width, (k + 1) * width)
                return w_hi[:, slot, w], w_lo[:, slot, w]

            def act_of(hi, lo, k, cols=slice(0, S)):
                return hi[:, k, cols], lo[:, k, cols]

            def column_part(slot, bank, hi, lo, cols, k_wait=None, ks=range(KC)):
                for k in ks:
                    if k_wait:
                        k_wait(k)
                    last = three(ps[:, bank, cols], wcol(slot, k), act_of(hi, lo, k, cols), k == 0, k == KC - 1)
                return last

            def column_tile(slot, n, bank, hi, lo, width=S, k_wait=None):
                pe.wait_ge(lo_ready, n + 1)
                column_part(slot, bank, hi, lo, slice(0, width), k_wait).then_inc(tile_done, 1)

            pe.wait_ge(ident_ready, 2)
            for _ in range(WARM):
                mm(ps[:, 7, 0:P], ident[:, :], ident[:, :], start=True, stop=True)

            def lru_gates(c, first):
                if not first:
                    pe.wait_ge(glru_ready, c)
                pe.wait_ge(lo_ready, 4 * c + N_L1 + 4)
                before = KC - 1 if first else 2
                column_part(3, 2, a_hi, a_lo, slice(0, S), ks=range(before))
                pe.wait_ge(ulo_ready, c + 1)
                if not first:
                    pe.wait_ge(ri_ready, 2 * c)
                for g in range(2):
                    last = three(ps[:, 4 + g, :], wcol(2, g), (u_hi[:, :], u_lo[:, :]), True, True)
                last.then_inc(tile_done, 1)
                column_part(3, 2, a_hi, a_lo, slice(0, S), ks=range(before, KC)).then_inc(tile_done, 1)

            HEAD_WAITS = {0: (head_lo, 2), 1: (lo_ready, 1), 2: (lo_ready, 3), 4: (lo_ready, 4), 6: (lo_ready, 5)}

            def head_wait(k):
                if k in HEAD_WAITS:
                    pe.wait_ge(*HEAD_WAITS[k])

            column_part(0, 0, a_hi, a_lo, slice(0, S), head_wait).then_inc(tile_done, 1)
            column_tile(1, 5, 1, a_hi, a_lo)
            lru_gates(0, True)
            with pe.Fori(1, KC) as c:
                pe.wait_ge(u_ready, c)
                column_tile(0, 4 * c + N_L1, 0, a_hi, a_lo)
                pe.wait_ge(ge_ready, c)
                column_tile(1, 4 * c + N_L1 + 1, 1, a_hi, a_lo)
                lru_gates(c, False)

            pe.wait_ge(u_ready, KC)
            pe.wait_ge(ge_ready, KC)
            pe.wait_ge(glru_ready, KC)
            for d in range(LRU_AHEAD):
                pe.wait_ge(lo_ready, N_L2 + d + 1)
                column_part(d, d, b_hi, b_lo, slice(0, S), (lambda k: pe.wait_ge(ghlo_ready, k + 1)) if d == 0 else None,
                            range(KC - 1))
            pe.wait_ge(ghlo_ready, KC)
            for d in range(LRU_AHEAD):
                column_part(d, d, b_hi, b_lo, slice(0, S), ks=range(KC - 1, KC)).then_inc(tile_done, 1)
            pe.wait_ge(ri_ready, 2 * KC)
            for d in range(LRU_AHEAD, KC):
                column_tile(d, N_L2 + d, d, b_hi, b_lo)

            def sc_chunk(c, first):
                for p, read in enumerate((cc_ready, prod_ready, sco_ready, gsc_ready)):
                    if first:
                        pe.wait_ge(ylru_read, p + 1)
                    else:
                        pe.wait_ge(read, c)
                    column_tile(p, 4 * c + N_L3 + p, p, a_hi, a_lo)

            sc_chunk(0, True)
            with pe.Fori(1, KC) as c:
                sc_chunk(c, False)

            for d in range(KC):
                if d < 4:
                    pe.wait_ge(ylru_read, 5 + d)
                else:
                    pe.wait_ge((cc_ready, prod_ready, sco_ready, gsc_ready)[d - 4], KC)
                column_tile(d, N_L4 + d, (d + 4) % 8, b_hi, b_lo,
                            k_wait=(lambda k: pe.wait_ge(sclo_ready, k + 1)) if d == 0 else None)

            def row_group(slots, n0, bank, hi, lo, cols, k_wait=None):
                for k in range(KC):
                    if k % 2 == 0 and n0 is not None:
                        pe.wait_ge(lo_ready, n0 + k // 2 + 1)
                    if k_wait:
                        k_wait(k)
                    last = three(ps[:, bank, :], act_of(hi, lo, k, cols),
                                 wcol(slots + k // 2, k % 2, HALF), k == 0, k == KC - 1)
                last.then_inc(group_done, 1)

            def turn(src, dst_bank, ks=range(KC)):
                o = bank2(dst_bank)
                for k in ks:
                    last = nc.tensor.transpose(o[:, k, :], src[:, k * P:(k + 1) * P], ident[:, :])
                return last

            for h in range(2):
                for t in range(ST):
                    pe.wait_ge(ysc_read, (5 if h == 0 else 1) + t)
                    row_group(4 * h, N_MIX + 4 * h if t == 0 else None, 4 * h + t, a_hi, a_lo,
                              slice(t * P, (t + 1) * P),
                              k_wait=(lambda k: pe.wait_ge(alo_ready, k + 1)) if h == t == 0 else None)

            for what, j in K_AND_TURNS:
                if what == "k":
                    if j < 4:
                        pe.wait_ge(pre_ready, (1, 2, 7, 8)[j])
                    else:
                        pe.wait_ge(klo_ready, j - 3)
                    column_tile(j, N_K + j, K_BANK[j % 4], m_hi, m_lo, NM)
                else:
                    pe.wait_ge(y_ready, j + 1)
                    if j < 2:
                        pe.wait_ge(pre_ready, 4 + 2 * j)
                    else:
                        pe.wait_ge(blo_ready, 2 * (j - 1))
                    turn(resid[:, j, :], TURN_BANK[j]).then_inc(turned, 1)

            pe.wait_ge(blo_ready, B_LN1)
            for j in range(KC):
                if j < 2:
                    pe.wait_ge(klo_ready, 5 + j)
                else:
                    pe.wait_ge(alo_ready, A_MERGED + j - 1)
                column_tile(j, N_Q + j, j % 2, b_hi, b_lo)

            def scores(t):
                if t == ST - 1:
                    pe.wait_ge(blo_ready, B_LN1 + 4)
                o = ps[:, S_BANK[t]:S_BANK[t] + 2, :].rearrange("p b (h m) -> p (b h) m", m=NM)
                for h in range(NH):
                    for j in range(2):
                        k = 2 * h + j
                        kt = slice(k * NM, (k + 1) * NM)
                        last = three(o[:, h, :], act_of(a_hi, a_lo, k, slice(t * P, (t + 1) * P)),
                                     (kv_hi[:, kt], kv_lo[:, kt]), j == 0, j == 1)
                last.then_inc(scores_done, 1)

            def v_group(g):
                h, m = g // 2, g % 2
                if g < 2:
                    pe.wait_ge(klo_ready, 7 + g)
                else:
                    pe.wait_ge(blo_ready, B_LN1 + 2)
                row_group(4 * h, N_V + 4 * h if m == 0 else None, V_BANK[g], m_hi, m_lo,
                          slice(m * P, (m + 1) * P))

            def turn_probs(t):
                pe.wait_ge(probs_ready, t + 1)
                turn(probs[:, t % 2, :], S_BANK[t]).then_inc(probs_turned, 1)

            v_group(0)
            pe.wait_ge(klo_ready, KC)
            pe.wait_ge(alo_ready, A_Q)
            scores(0)
            scores(1)
            v_group(1)
            turn_probs(0)
            turn_probs(1)
            scores(2)
            scores(3)
            v_group(2)
            turn_probs(2)
            turn_probs(3)
            v_group(3)

            pe.wait_ge(blo_ready, B_P)
            for g in range(KC):
                if g < 4:
                    pe.wait_ge(vlo_ready, max(2, g + 1))
                else:
                    pe.wait_ge(alo_ready, A_Q + g - 3)
                h, dc = g // 2, g % 2
                for m in range(2):
                    vc = slice(m * D + h * HD + dc * P, m * D + h * HD + (dc + 1) * P)
                    last = three(ps[:, V_BANK[g % 4], :], (kv_hi[:, vc], kv_lo[:, vc]),
                                 act_of(b_hi, b_lo, 2 * h + m), m == 0, m == 1)
                last.then_inc(att_done, 1)

            def xo_group(h, t):
                if h == 1:
                    pe.wait_ge(alo_ready, A_Q + 5 + t)
                row_group(4 * h, N_XO + 4 * h if t == 0 else None, (V_BANK if h else XO_BANK)[t], a_hi, a_lo,
                          slice(t * P, (t + 1) * P),
                          k_wait=(lambda k: pe.wait_ge(alo_ready, A_Q + k + 1)) if h == t == 0 else None)

            def turn_ln2(t):
                if t < ST - 1:
                    pe.wait_ge(pre_ready, 2 * ST + (2, 4, ST + 2)[t])
                else:
                    pe.wait_ge(blo_ready, B_P + 4)
                pe.wait_ge(y_ready, ST + t + 1 + (t == ST - 1))
                turn(resid[:, t, :], LN2_BANK[t]).then_inc(turned, 1)

            for t in range(ST):
                xo_group(0, t)
            xo_group(1, 0)
            xo_group(1, 1)
            xo_group(1, 2)
            turn_ln2(0)
            turn_ln2(1)
            xo_group(1, 3)
            turn_ln2(2)

            UP_N = (0, 1, 2, 3, 5, 6, 8, 9)
            DOWN_N = (4, 7, 10, 11)

            def ffn_pair(q, j, first):
                if not (first and j < 2):
                    pe.wait_ge(cg_ready, 4 * q + j - 1)
                column_tile((2 * j) % 4, 12 * q + N_FFN + UP_N[2 * j], j % 2, b_hi, b_lo)
                if not (first and j < 2):
                    pe.wait_ge(hf_ready, 4 * q + j - 1)
                column_tile((2 * j + 1) % 4, 12 * q + N_FFN + UP_N[2 * j + 1], 2 + j % 2, b_hi, b_lo)

            def ffn_first_pair():
                pe.wait_ge(blo_ready, B_P + 4)
                pe.wait_ge(lo_ready, N_FFN + 2)
                column_part(0, 0, b_hi, b_lo, slice(0, 2 * P))
                pe.wait_ge(pre_ready, 3 * ST + 3)
                column_part(1, 2, b_hi, b_lo, slice(0, 2 * P))
                turn_ln2(3)
                pe.wait_ge(blo_ready, B_P + 6)
                column_part(0, 0, b_hi, b_lo, slice(2 * P, 3 * P))
                pe.wait_ge(blo_ready, B_LN2)
                column_part(0, 0, b_hi, b_lo, slice(3 * P, S)).then_inc(tile_done, 1)
                column_part(1, 2, b_hi, b_lo, slice(2 * P, S)).then_inc(tile_done, 1)

            def down(q, g, j):
                t, h = g // 2, g % 2
                return three(ps[:, 4 + g % 4, :], act_of(a_hi, a_lo, j, slice(t * P, (t + 1) * P)),
                             wcol(4 + j, h, HALF), j == 0, j == SEG - 1)

            def ffn_segment(q, first):
                for j in range(SEG):
                    if first and j == 0:
                        ffn_first_pair()
                    else:
                        ffn_pair(q, j, first)
                pe.wait_ge(lo_ready, 12 * q + N_FFN + SEG_TILES)
                for g in range(2):
                    if not first:
                        pe.wait_ge(acc_ready, 8 * q + g - 3)
                    for j in range(SEG - 1):
                        if g == 0:
                            pe.wait_ge(hlo_ready, 4 * q + j + 1)
                        down(q, g, j)
                pe.wait_ge(hlo_ready, 4 * q + SEG)
                for g in range(2):
                    down(q, g, SEG - 1).then_inc(group_done, 1)
                for g in range(2, 2 * ST):
                    if not (first and g < 4):
                        pe.wait_ge(acc_ready, 8 * q + g - 3)
                    for j in range(SEG):
                        last = down(q, g, j)
                    last.then_inc(group_done, 1)

            ffn_segment(0, True)
            with pe.Fori(1, NSEG) as q:
                ffn_segment(q, False)

        @block.scalar
        def _(act):
            fn = nc.scalar.activation

            def split_hi(n, rslot, dst, free=None, width=TW):
                if free:
                    act.wait_ge(free[0], free[1])
                act.wait_ge(raw_loaded[rslot], 16 * (n // RAW) + 16 if isinstance(n, int) else 4 * (n - rslot) + 16)
                fn(dst, raw[:, rslot, 0:width], ACT.Copy).then_inc(hi_ready, 1)

            def w_split(n, rslot, slot, free=None, width=TW):
                split_hi(n, rslot, w_hi[:, slot, 0:width], free, width)

            def col(base, c):
                return par[:, base:base + KC][:, bass.ds(c, 1)]

            def dcol(base, c):
                return der[:, base:base + KC][:, bass.ds(c, 1)]

            def x_part(i):
                return a_hi[:, 2 * i:2 * i + 2, :].rearrange("p k s -> p (k s)")

            act.dma_start(par[:, :], params).then_inc(par_loaded, 16)
            act.wait_ge(head_loaded, 32)
            fn(a_hi[:, 0, :], raw[:, 0, 0:HALF], ACT.Copy).then_inc(head_hi, 1)
            fn(w_hi[:, 0, 0:HALF], raw[:, 1, 0:HALF], ACT.Copy).then_inc(head_hi, 1)
            act.wait_ge(raw_loaded[0], 16)
            fn(a_hi[:, 1, :], raw[:, 0, HALF:TW], ACT.Copy).then_inc(hi_ready, 1)
            act.wait_ge(raw_loaded[1], 16)
            fn(w_hi[:, 0, HALF:TW], raw[:, 1, HALF:TW], ACT.Copy).then_inc(hi_ready, 1)
            split_hi(2, 2, x_part(1))
            split_hi(3, 3, x_part(2))
            split_hi(4, 0, x_part(3))
            w_split(5, 1, 1)
            w_split(6, 2, 2, width=2 * P)

            def lru_decay(c):
                act.wait_ge(guard_ready, c + 1)
                fn(dec[:, :], t_r[:, :], ACT.Exp, scale=dcol(D_NC4, c), bias=dcol(D_NC4, c)).then_inc(dec_ready, 1)
                fn(mult[:, 1:S], t_r[:, 1:S], ACT.Tanh, scale=dcol(D_C4, c), bias=dcol(D_C4, c)).then_inc(th_ready, 1)

            def lru_sqrt(c):
                act.wait_ge(m2_ready, c + 1)
                fn(mult[:, 1:S], mult[:, 1:S], ACT.Sqrt).then_inc(mult_ready, 1)

            def lru_conv0(c, first):
                if not first:
                    act.wait_ge(iu_ready, c)
                act.wait_ge(tile_done, 4 * c + 1)
                fn(u[:, :], ps[:, 0, :], ACT.Identity, scale=col(C_CW, c), bias=col(C_CB, c)).then_inc(conv0_ready, 1)

            def lru_out_hi(c):
                act.wait_ge(gh_ready, c + 1)
                fn(b_hi[:, c, :], hst[:, :], ACT.Copy).then_inc(ghhi_ready, 1)

            def lru_chunk(c, first, last):
                w_split(4 * c + N_L1 + 3, 3, 3, None if first else (tile_done, 4 * c))
                if first:
                    act.wait_ge(par_loaded, 16)
                else:
                    lru_out_hi(c - 1)
                lru_conv0(c, first)
                if first:
                    act.wait_ge(prep, 3)
                    fn(setup[:, 16:24], setup[:, 8:16], ACT.Exp).then_inc(prep_exp, 1)
                w_split(4 * c + N_L1 + 4, 0, 0, (tile_done, 4 * c + 1))
                act.wait_ge(u_ready, c + 1)
                fn(u_hi[:, :], u[:, :], ACT.Copy).then_inc(uhi_ready, 1)
                act.wait_ge(tile_done, 4 * c + 2)
                fn(gpoly[:, :], ps[:, 1, :], ACT.Square).then_inc(gsq_ready, 1)
                w_split(4 * c + N_L1 + 5, 1, 1, (tile_done, 4 * c + 2))
                act.wait_ge(gp2_ready, c + 1)
                fn(gth[:, :], gpoly[:, :], ACT.Tanh, scale=GELU_C).then_inc(gth_ready, 1)
                if first:
                    act.wait_ge(prep, PREP_STEPS)
                act.wait_ge(tile_done, 4 * c + 3)
                fn(t_r[:, :], ps[:, 4, :], ACT.Tanh, scale=0.5, bias=dcol(D_HBR, c)).then_inc(ri_ready, 1)
                fn(t_i[:, :], ps[:, 5, :], ACT.Tanh, scale=0.5, bias=dcol(D_HBI, c)).then_inc(ri_ready, 1)
                lru_decay(c)
                w_split(4 * c + N_L1 + 6, 2, 2, (tile_done, 4 * c + 3), TW if last else 2 * P)
                lru_sqrt(c)
                act.wait_ge(tile_done, 4 * c + 4)
                fn(side1[:, c, :], ps[:, 2, :], ACT.Tanh, scale=0.5, bias=dcol(D_HBM, c)).then_inc(glru_ready, 1)

            lru_chunk(0, True, False)
            with act.Fori(1, KC - 1) as c:
                lru_chunk(c, False, False)
            lru_chunk(KC - 1, False, True)
            w_split(N_L2 + 3, 3, 3, (tile_done, T_L2))
            lru_out_hi(KC - 1)

            for d in range(1, KC):
                n = N_L2 + d + 3
                if d + 3 < KC:
                    w_split(n, n % 4, d + 3)
                else:
                    w_split(n, n % 4, d + 3 - KC, (tile_done, T_L2 + d + 3 - KC + 1))

            def sc_chunk(c, first):
                t = 4 * c + T_L3
                w_split(4 * c + N_L3 + 3, 3, 3, (tile_done, t if not first else T_L2 + 4))
                if not first:
                    act.wait_ge(prod_ready, c)
                act.wait_ge(tile_done, t + 1)
                fn(cc[:, :], ps[:, 0, :], ACT.Copy).then_inc(cc_ready, 1)
                w_split(4 * c + N_L3 + 4, 0, 0, (tile_done, t + 1))
                act.wait_ge(prod_ready, c + 1)
                fn(cv[:, :], prod[:, :], ACT.Copy, scale=col(C_SW, c)).then_inc(cv0_ready, 1)
                w_split(4 * c + N_L3 + 5, 1, 1, (tile_done, t + 2))
                act.wait_ge(sco_ready, c + 1)
                fn(b_hi[:, c, :], sco[:, :], ACT.Copy).then_inc(schi_ready, 1)
                w_split(4 * c + N_L3 + 6, 2, 2, (tile_done, t + 3))
                act.wait_ge(tile_done, t + 4)
                fn(side2[:, c, :], ps[:, 3, :], ACT.Tanh, scale=0.5, bias=dcol(D_HBM + 8, c)).then_inc(gsc_ready, 1)

            sc_chunk(0, True)
            with act.Fori(1, KC) as c:
                sc_chunk(c, False)

            for d in range(KC):
                n = N_L4 + d + 3
                if d == 0:
                    w_split(n, n % 4, 3, (tile_done, T_L4))
                elif d + 3 < KC:
                    w_split(n, n % 4, d + 3)
                else:
                    w_split(n, n % 4, d + 3 - KC, (tile_done, T_L4 + d + 3 - KC + 1))
                act.wait_ge(merged_ready, d + 1)
                fn(a_hi[:, d, :], (sco if d % 2 else cv)[:, :], ACT.Copy, scale=0.5).then_inc(ahi_ready, 1)

            w_split(N_MIX + 3, 3, 3, (tile_done, T_L4 + 4))
            for j in range(4):
                w_split(N_MIX + 4 + j, j, 4 + j, (tile_done, T_L4 + 5 + j))
            act.wait_ge(alo_ready, A_MERGED)
            for i in range(2):
                act.dma_start(rows1[:, i, :], lnrows[i:i + 1, :].broadcast_to([P, D])).then_inc(rows_loaded, 16)

            def ln_sqrt(i):
                act.wait_ge(var_ready, i + 1)
                t = i % ST
                fn(rstd[:, t, 1:2], rstd[:, t, 0:1], ACT.Sqrt).then_inc(rstd_ready, 1)

            for j in range(4):
                split_hi(N_MEM + j, j, m_hi[:, 2 * j:2 * j + 2, :].rearrange("p k m -> p (k m)"), width=2 * NM)
            for j in range(4):
                w_split(N_K + j, j, j, (group_done, 4))
                ln_sqrt(j)

            def turned_hi(bank, t, half):
                fn(b_hi[:, 4 * half:4 * half + 4, t * P:(t + 1) * P],
                   bank2(bank)[:, 4 * half:4 * half + 4, :], ACT.Copy).then_inc(bhi_ready, 1)

            for what, j in K_AND_TURNS:
                if what == "k":
                    if j < 4:
                        w_split(N_K + 4 + j, j, 4 + j, (group_done, 8))
                    else:
                        w_split(N_Q + j - 4, j - 4, j - 4, (tile_done, T_K + j - 3))
                    act.wait_ge(tile_done, T_K + j + 1)
                    fn(kv_hi[:, j * NM:(j + 1) * NM], ps[:, K_BANK[j % 4], 0:NM], ACT.Copy).then_inc(khi_ready, 1)
                else:
                    act.wait_ge(turned, j + 1)
                    for half in range(2):
                        turned_hi(TURN_BANK[j], j, half)
            for j in range(KC):
                if j < 4:
                    w_split(N_Q + 4 + j, j, 4 + j, (tile_done, T_K + 5 + j))
                else:
                    w_split(N_V + j - 4, j - 4, j - 4, (tile_done, T_Q + j - 3))
                act.wait_ge(tile_done, T_Q + j + 1)
                fn(a_hi[:, j, :], ps[:, j % 2, :], ACT.Copy).then_inc(ahi_ready, 1)

            def exps(t):
                act.wait_ge(negmax_ready, t + 1)
                if t >= 2:
                    act.wait_ge(probs_turned, t - 1)
                o = ps[:, S_BANK[t]:S_BANK[t] + 2, :].rearrange("p b (h m) -> p (b h) m", m=NM)
                for h in range(NH):
                    fn(probs[:, t % 2, h * NM:(h + 1) * NM], o[:, h, :], ACT.Exp, scale=HD ** -0.5,
                       bias=mx[:, t % 2, h:h + 1], accum_out=sums[:, t % 2, h:h + 1]).then_inc(exp_ready, 1)

            def probs_hi(t):
                act.wait_ge(probs_turned, t + 1)
                for half in range(2):
                    turned_hi(S_BANK[t], t, half)

            def v_hi(g):
                h, m = g // 2, g % 2
                act.wait_ge(group_done, G_V + g + 1)
                fn(kv_hi[:, m * D + h * HALF:m * D + (h + 1) * HALF], ps[:, V_BANK[g], :],
                   ACT.Copy).then_inc(vhi_ready, 1)

            for j in range(4):
                w_split(N_V + 4 + j, j, 4 + j, (tile_done, T_Q + 5 + j))
            exps(0)
            exps(1)
            probs_hi(0)
            probs_hi(1)
            exps(2)
            exps(3)
            act.wait_ge(scores_done, 4)
            v_hi(0)
            v_hi(1)
            probs_hi(2)
            probs_hi(3)
            w_split(N_XO, 0, 0, (group_done, G_V + 2))
            v_hi(2)
            w_split(N_XO + 1, 1, 1)
            w_split(N_XO + 2, 2, 2)
            v_hi(3)
            w_split(N_XO + 3, 3, 3)
            for g in range(KC):
                if g < 4:
                    w_split(N_XO + 4 + g, g, 4 + g, (group_done, G_XO))
                act.wait_ge(att_done, g + 1)
                fn(a_hi[:, g, :], ps[:, V_BANK[g % 4], :], ACT.Copy).then_inc(ahi_ready, 1)
            act.wait_ge(probs_turned, ST)
            for i in range(2):
                act.dma_start(rows2[:, i, :], lnrows[2 + i:3 + i, :].broadcast_to([P, D])).then_inc(rows_loaded, 16)
            for i in range(2):
                act.dma_start(rows3[:, i, :], lnrows[4 + i:5 + i, :].broadcast_to([P, D])).then_inc(rows_loaded, 16)
            for j in range(3):
                w_split(N_FFN + j, j, j, (group_done, G_XO + 4))
                ln_sqrt(ST + j)

            def ln2_hi(t):
                act.wait_ge(turned, ST + t + 1)
                for half in range(2):
                    turned_hi(LN2_BANK[t], t, half)

            ln2_hi(0)
            ln2_hi(1)
            w_split(N_FFN + 3, 3, 3)
            ln_sqrt(ST + 3)
            ln2_hi(2)
            ln2_hi(3)

            def ffn_segment(q, last):
                n, t = 12 * q + N_FFN, 8 * q + T_FFN

                def prm(i):
                    return par[:, bass.ds(16 * q + (C_FF + i), 1)]

                def conv0(j):
                    act.wait_ge(tile_done, t + 2 * j + 1)
                    fn(cg[:, :], ps[:, j % 2, :], ACT.Identity, scale=prm(j), bias=prm(12 + j)).then_inc(cg0_ready, 1)

                def gelu(j):
                    act.wait_ge(cg_ready, 4 * q + j + 1)
                    fn(fg[:, :], cg[:, :], ACT.Gelu_apprx_tanh).then_inc(fg_ready, 1)

                def h_hi(j):
                    act.wait_ge(hf_ready, 4 * q + j + 1)
                    fn(a_hi[:, j, :], hf[:, :], ACT.Copy).then_inc(hhi_ready, 1)

                w_split(n + 4, 0, 4, (group_done, 8 * q + G_FFN))
                conv0(0)
                w_split(n + 5, 1, 0, (tile_done, t + 1))
                gelu(0)
                w_split(n + 6, 2, 1, (tile_done, t + 2))
                h_hi(0)
                w_split(n + 7, 3, 5)
                conv0(1)
                w_split(n + 8, 0, 2, (tile_done, t + 3))
                gelu(1)
                w_split(n + 9, 1, 3, (tile_done, t + 4))
                h_hi(1)
                w_split(n + 10, 2, 6)
                conv0(2)
                w_split(n + 11, 3, 7)
                gelu(2)
                h_hi(2)
                conv0(3)
                gelu(3)
                h_hi(3)
                if not last:
                    for p in range(4):
                        w_split(n + 12 + p, p, p, (tile_done, t + 5 + p))

            with act.Fori(0, NSEG - 1) as q:
                ffn_segment(q, False)
            ffn_segment(NSEG - 1, True)
            for j in range(ST):
                ln_sqrt(2 * ST + j)

        @block.vector
        def _(dve):
            v = nc.vector

            def split_lo(n, rslot, hi, lo, width=TW):
                dve.wait_ge(hi_ready, n + 1)
                v.tensor_tensor(lo, raw[:, rslot, 0:width], hi.bitcast(F32), ALU.subtract).then_inc(lo_ready, 1)

            def w_split(n, rslot, slot, width=TW):
                split_lo(n, rslot, w_hi[:, slot, 0:width], w_lo[:, slot, 0:width], width)

            def col(base, c):
                return par[:, base:base + KC][:, bass.ds(c, 1)]

            def x_split(n, rslot, i):
                hi, lo = (z[:, 2 * i:2 * i + 2, :].rearrange("p k s -> p (k s)") for z in (a_hi, a_lo))
                split_lo(n, rslot, hi, lo)

            def prep_steps():
                neg, nabs, z, den, rec, s, s2, pl = (setup[:, 8 * i:8 * i + 8] for i in range(8))
                lam = par[:, C_LAM:C_LAM + 8]
                yield lambda: v.tensor_scalar(neg, lam, -1.0, None, ALU.mult)
                yield lambda: v.tensor_tensor(nabs, lam, neg, ALU.min)
                yield lambda: v.tensor_scalar(neg, neg, 0.0, None, ALU.max)
                yield lambda: v.tensor_scalar(den, z, 2.0, None, ALU.add)
                yield lambda: v.reciprocal(rec, den)
                yield lambda: v.tensor_tensor(s, z, rec, ALU.mult)
                yield lambda: v.tensor_tensor(s2, s, s, ALU.mult)
                yield lambda: v.tensor_scalar(pl, s2, 1.0 / 17, None, ALU.mult)
                for m in (15, 13, 11, 9, 7, 5, 3):
                    yield lambda m=m: v.scalar_tensor_tensor(pl, pl, 1.0 / m, s2, ALU.add, ALU.mult)
                yield lambda: v.scalar_tensor_tensor(pl, pl, 1.0, s, ALU.add, ALU.mult)
                yield lambda: v.scalar_tensor_tensor(pl, pl, 2.0, neg, ALU.mult, ALU.add)
                yield lambda: v.tensor_scalar(der[:, D_C4:D_C4 + 8], pl, 4.0, None, ALU.mult)
                yield lambda: v.tensor_scalar(der[:, D_NC4:D_NC4 + 8], pl, -4.0, None, ALU.mult)
                yield lambda: v.tensor_scalar(der[:, D_HBR:D_HBR + 16], par[:, C_BR:C_BR + 16], 0.5, None, ALU.mult)
                yield lambda: v.tensor_scalar(der[:, D_HBM:D_HBM + 16], par[:, C_BM:C_BM + 16], 0.5, None, ALU.mult)

            dve.wait_ge(head_hi, 1)
            v.tensor_tensor(a_lo[:, 0, :], raw[:, 0, 0:HALF], a_hi[:, 0, :].bitcast(F32), ALU.subtract).then_inc(head_lo, 1)
            dve.wait_ge(head_hi, 2)
            v.tensor_tensor(w_lo[:, 0, 0:HALF], raw[:, 1, 0:HALF], w_hi[:, 0, 0:HALF].bitcast(F32),
                            ALU.subtract).then_inc(head_lo, 1)
            dve.wait_ge(hi_ready, 1)
            v.tensor_tensor(a_lo[:, 1, :], raw[:, 0, HALF:TW], a_hi[:, 1, :].bitcast(F32), ALU.subtract).then_inc(lo_ready, 1)
            dve.wait_ge(hi_ready, 2)
            v.tensor_tensor(w_lo[:, 0, HALF:TW], raw[:, 1, HALF:TW], w_hi[:, 0, HALF:TW].bitcast(F32),
                            ALU.subtract).then_inc(lo_ready, 1)
            x_split(2, 2, 1)
            x_split(3, 3, 2)
            x_split(4, 0, 3)
            w_split(5, 1, 1)
            w_split(6, 2, 2, 2 * P)
            v.memset(mult[:, 0:1], 1.0).then_inc(one_ready, 1)
            prep_list = list(prep_steps())

            def prepare(lo, hi):
                for i in range(lo, hi):
                    if i:
                        dve.wait_ge(prep, i)
                    if i == 3:
                        dve.wait_ge(prep_exp, 1)
                    prep_list[i]().then_inc(prep, 1)

            dve.wait_ge(par_loaded, 16)
            prepare(0, 3)

            def lru_m2(c):
                dve.wait_ge(decsq_ready, c + 1)
                dve.wait_ge(th_ready, c + 1)
                v.scalar_tensor_tensor(mult[:, 1:S], decsq[:, 1:S], 1.0, mult[:, 1:S], ALU.add, ALU.mult).then_inc(m2_ready, 1)

            def lru_scan(c):
                dve.wait_ge(mult_ready, c + 1)
                v.tensor_tensor(binp[:, :], binp[:, :], mult[:, :], ALU.mult).then_inc(b_ready, 1)
                dve.wait_ge(b_ready, c + 1)
                v.tensor_tensor_scan(hst[:, :], dec[:, :], binp[:, :], 0.0, ALU.mult, ALU.add).then_inc(h_ready, 1)
                dve.wait_ge(h_ready, c + 1)
                v.scalar_tensor_tensor(hst[:, :], ge[:, :], 0.25, hst[:, :], ALU.mult, ALU.mult).then_inc(gh_ready, 1)

            def lru_out_lo(c):
                dve.wait_ge(ghhi_ready, c + 1)
                v.tensor_tensor(b_lo[:, c, :], hst[:, :], b_hi[:, c, :].bitcast(F32), ALU.subtract).then_inc(ghlo_ready, 1)

            def lru_taps(c):
                dve.wait_ge(conv0_ready, c + 1)
                for k in range(1, 4):
                    if k > 1:
                        dve.wait_ge(taps, 2 * c + k - 1)
                    tap = v.scalar_tensor_tensor(u[:, k:S], ps[:, 0, 0:S - k], col(C_CW + 8 * k, c), u[:, k:S],
                                                 ALU.mult, ALU.add)
                    tap.then_inc(taps if k < 3 else u_ready, 1)

            def lru_chunk(c, first, last):
                w_split(4 * c + N_L1 + 3, 3, 3)
                if not first:
                    lru_out_lo(c - 1)
                lru_taps(c)
                w_split(4 * c + N_L1 + 4, 0, 0)
                dve.wait_ge(uhi_ready, c + 1)
                v.tensor_tensor(u_lo[:, :], u[:, :], u_hi[:, :].bitcast(F32), ALU.subtract).then_inc(ulo_ready, 1)
                if first:
                    prepare(3, PREP_STEPS)
                dve.wait_ge(gsq_ready, c + 1)
                v.tensor_scalar(gpoly[:, :], gpoly[:, :], GELU_A, 1.0, ALU.mult, ALU.add).then_inc(gp1_ready, 1)
                dve.wait_ge(gp1_ready, c + 1)
                v.tensor_tensor(gpoly[:, :], gpoly[:, :], ps[:, 1, :], ALU.mult).then_inc(gp2_ready, 1)
                w_split(4 * c + N_L1 + 5, 1, 1)
                dve.wait_ge(gth_ready, c + 1)
                v.scalar_tensor_tensor(ge[:, :], gth[:, :], 1.0, ps[:, 1, :], ALU.add, ALU.mult).then_inc(ge_ready, 1)
                dve.wait_ge(ri_ready, 2 * c + 1)
                v.tensor_scalar(t_r[:, :], t_r[:, :], -1.0, None, ALU.max).then_inc(guard_ready, 1)
                dve.wait_ge(ri_ready, 2 * c + 2)
                v.scalar_tensor_tensor(binp[:, :], t_i[:, :], 1.0, u[:, :], ALU.add, ALU.mult).then_inc(iu_ready, 1)
                w_split(4 * c + N_L1 + 6, 2, 2, TW if last else 2 * P)
                lru_m2(c)
                dve.wait_ge(iu_ready, c + 1)
                lru_scan(c)

            dve.wait_ge(one_ready, 1)
            lru_chunk(0, True, False)
            with dve.Fori(1, KC - 1) as c:
                lru_chunk(c, False, False)
            lru_chunk(KC - 1, False, True)
            w_split(N_L2 + 3, 3, 3)
            lru_out_lo(KC - 1)

            for d in range(KC):
                if d:
                    n = N_L2 + d + 3
                    w_split(n, n % 4, (d + 3) % 8)
                dve.wait_ge(tile_done, T_L2 + d + 1)
                dve.wait_ge(glru_ready, KC)
                v.scalar_tensor_tensor(side1[:, d, :], side1[:, d, :], 1.0, ps[:, d, :], ALU.add,
                                       ALU.mult).then_inc(ylru_read, 1)

            def sc_chunk(c):
                w_split(4 * c + N_L3 + 3, 3, 3)
                dve.wait_ge(cc_ready, c + 1)
                dve.wait_ge(tile_done, 4 * c + T_L3 + 2)
                v.tensor_tensor(prod[:, :], cc[:, :], ps[:, 1, :], ALU.mult).then_inc(prod_ready, 1)
                w_split(4 * c + N_L3 + 4, 0, 0)
                dve.wait_ge(cv0_ready, c + 1)
                v.scalar_tensor_tensor(cv[:, 1:S], prod[:, 0:S - 1], col(C_SW + 8, c), cv[:, 1:S], ALU.mult,
                                       ALU.add).then_inc(sctap, 1)
                dve.wait_ge(sctap, c + 1)
                v.scalar_tensor_tensor(cv[:, 2:S], prod[:, 0:S - 2], col(C_SW + 16, c), cv[:, 2:S], ALU.mult,
                                       ALU.add).then_inc(cv_ready, 1)
                w_split(4 * c + N_L3 + 5, 1, 1)
                dve.wait_ge(cv_ready, c + 1)
                dve.wait_ge(tile_done, 4 * c + T_L3 + 3)
                v.tensor_tensor(sco[:, :], cv[:, :], ps[:, 2, :], ALU.mult).then_inc(sco_ready, 1)
                w_split(4 * c + N_L3 + 6, 2, 2)
                dve.wait_ge(schi_ready, c + 1)
                v.tensor_tensor(b_lo[:, c, :], sco[:, :], b_hi[:, c, :].bitcast(F32), ALU.subtract).then_inc(sclo_ready, 1)

            with dve.Fori(0, KC) as c:
                sc_chunk(c)

            dve.wait_ge(gsc_ready, KC)
            dve.wait_ge(ylru_read, KC)
            for d in range(KC):
                buf = (sco if d % 2 else cv)
                dve.wait_ge(tile_done, T_L4 + d + 1)
                if d >= 2:
                    dve.wait_ge(alo_ready, d - 1)
                v.scalar_tensor_tensor(buf[:, :], side2[:, d, :], 1.0, ps[:, (d + 4) % 8, :], ALU.add,
                                       ALU.mult).then_inc(ysc_read, 1)
                dve.wait_ge(ysc_read, d + 1)
                v.tensor_tensor(buf[:, :], buf[:, :], side1[:, d, :], ALU.add).then_inc(merged_ready, 1)
                n = N_L4 + d + 3
                w_split(n, n % 4, (d + 3) % 8)
                dve.wait_ge(ahi_ready, d + 1)
                v.scalar_tensor_tensor(a_lo[:, d, :], buf[:, :], 0.5, a_hi[:, d, :].bitcast(F32), ALU.mult,
                                       ALU.subtract).then_inc(alo_ready, 1)

            steps = [0]

            def step(ins):
                ins.then_inc(ln, 1)
                steps[0] += 1
                dve.wait_ge(ln, steps[0])

            pres = [0]

            def pre(t, h, bank, group, scale):
                cols = slice(h * HALF, (h + 1) * HALF)
                dve.wait_ge(group_done, group + 1)
                v.scalar_tensor_tensor(resid[:, t, cols], resid[:, t, cols], scale, ps[:, bank, :], ALU.mult,
                                       ALU.add).then_inc(pre_ready, 1)
                pres[0] += 1
                dve.wait_ge(pre_ready, pres[0])
                step(v.bn_stats(stats[:, t, h, :], resid[:, t, cols]))

            def layer_norm(i, t, rows, halves):
                step(v.bn_aggr(mv[:, t, :], stats[:, t, :, :].rearrange("p h s -> p (h s)")))
                step(v.tensor_scalar(rstd[:, t, 0:1], mv[:, t, 1:2], EPS, None, ALU.add))
                v.reciprocal(rstd[:, t, 0:1], rstd[:, t, 0:1]).then_inc(var_ready, 1)
                parts = [slice(h * D // halves, (h + 1) * D // halves) for h in range(halves)]
                for cols in parts:
                    centred = v.scalar_tensor_tensor(resid[:, t, cols], resid[:, t, cols], mv[:, t, 0:1],
                                                     rows[:, 0, cols], ALU.subtract, ALU.mult)
                step(centred)
                dve.wait_ge(rstd_ready, i + 1)
                for cols in parts:
                    v.scalar_tensor_tensor(resid[:, t, cols], resid[:, t, cols], rstd[:, t, 1:2], rows[:, 1, cols],
                                           ALU.mult, ALU.add).then_inc(y_ready, 1)

            def turned_lo(bank, t, half, count):
                dve.wait_ge(bhi_ready, count)
                v.tensor_tensor(b_lo[:, 4 * half:4 * half + 4, t * P:(t + 1) * P],
                                bank2(bank)[:, 4 * half:4 * half + 4, :],
                                b_hi[:, 4 * half:4 * half + 4, t * P:(t + 1) * P].bitcast(F32),
                                ALU.subtract).then_inc(blo_ready, 1)

            w_split(N_MIX + 3, 3, 3)
            dve.wait_ge(x_loaded, 16 * ST)
            for j in range(4):
                w_split(N_MIX + 4 + j, j, 4 + j)
                pre(j, 0, j, j, ALPHA)
            for j in range(4):
                split_lo(N_MEM + j, j, m_hi[:, 2 * j:2 * j + 2, :].rearrange("p k m -> p (k m)"),
                         m_lo[:, 2 * j:2 * j + 2, :].rearrange("p k m -> p (k m)"), 2 * NM)
            dve.wait_ge(rows_loaded, 32)
            for j in range(4):
                w_split(N_K + j, j, j)
                pre(j, 1, 4 + j, 4 + j, ALPHA)
                layer_norm(j, j, rows1, 1)
            for what, j in K_AND_TURNS:
                if what == "k":
                    if j < 4:
                        w_split(N_K + 4 + j, j, 4 + j)
                    else:
                        w_split(N_Q + j - 4, j - 4, j - 4)
                    dve.wait_ge(khi_ready, j + 1)
                    cols = slice(j * NM, (j + 1) * NM)
                    v.tensor_tensor(kv_lo[:, cols], ps[:, K_BANK[j % 4], 0:NM], kv_hi[:, cols].bitcast(F32),
                                    ALU.subtract).then_inc(klo_ready, 1)
                else:
                    for half in range(2):
                        turned_lo(TURN_BANK[j], j, half, 2 * j + half + 1)
            for j in range(KC):
                if j < 4:
                    w_split(N_Q + 4 + j, j, 4 + j)
                else:
                    w_split(N_V + j - 4, j - 4, j - 4)
                dve.wait_ge(ahi_ready, A_MERGED + j + 1)
                v.tensor_tensor(a_lo[:, j, :], ps[:, j % 2, :], a_hi[:, j, :].bitcast(F32),
                                ALU.subtract).then_inc(alo_ready, 1)

            def row_max(t):
                dve.wait_ge(scores_done, t + 1)
                if t >= 2:
                    dve.wait_ge(exp_ready, NH * (t - 1))
                o = ps[:, S_BANK[t]:S_BANK[t] + 2, :].rearrange("p b (h m) -> p (b h) m", m=NM)
                v.tensor_reduce(mx[:, t % 2, :], o, AX.X, ALU.max).then_inc(max_ready, 1)
                dve.wait_ge(max_ready, t + 1)
                v.tensor_scalar(mx[:, t % 2, :], mx[:, t % 2, :], -(HD ** -0.5), None, ALU.mult).then_inc(negmax_ready, 1)

            def normalise(t):
                dve.wait_ge(exp_ready, NH * (t + 1))
                v.reciprocal(sums[:, t % 2, :], sums[:, t % 2, :]).then_inc(rsum_ready, 1)
                dve.wait_ge(rsum_ready, t + 1)
                for h in range(NH):
                    cols = slice(h * NM, (h + 1) * NM)
                    last = v.tensor_scalar(probs[:, t % 2, cols], probs[:, t % 2, cols], sums[:, t % 2, h:h + 1],
                                           None, ALU.mult)
                last.then_inc(probs_ready, 1)

            def v_lo(g):
                h, m = g // 2, g % 2
                cols = slice(m * D + h * HALF, m * D + (h + 1) * HALF)
                dve.wait_ge(vhi_ready, g + 1)
                v.tensor_tensor(kv_lo[:, cols], ps[:, V_BANK[g], :], kv_hi[:, cols].bitcast(F32),
                                ALU.subtract).then_inc(vlo_ready, 1)

            def probs_lo(t):
                for half in range(2):
                    turned_lo(S_BANK[t], t, half, B_LN1 + 2 * t + half + 1)

            for j in range(4):
                w_split(N_V + 4 + j, j, 4 + j)
            row_max(0)
            row_max(1)
            normalise(0)
            normalise(1)
            probs_lo(0)
            probs_lo(1)
            row_max(2)
            row_max(3)
            normalise(2)
            normalise(3)
            v_lo(0)
            v_lo(1)
            probs_lo(2)
            probs_lo(3)
            w_split(N_XO, 0, 0)
            v_lo(2)
            w_split(N_XO + 1, 1, 1)
            w_split(N_XO + 2, 2, 2)
            v_lo(3)
            w_split(N_XO + 3, 3, 3)
            for g in range(KC):
                if g < 4:
                    w_split(N_XO + 4 + g, g, 4 + g)
                dve.wait_ge(ahi_ready, A_Q + g + 1)
                v.tensor_tensor(a_lo[:, g, :], ps[:, V_BANK[g % 4], :], a_hi[:, g, :].bitcast(F32),
                                ALU.subtract).then_inc(alo_ready, 1)
            for j in range(ST):
                pre(j, 0, XO_BANK[j], G_XO + j, ALPHA)
            dve.wait_ge(rows_loaded, 32 + 64)

            def ln2_lo(t):
                for half in range(2):
                    turned_lo(LN2_BANK[t], t, half, B_P + 2 * t + half + 1)

            for j in range(ST):
                if j < 3:
                    w_split(N_FFN + j, j, j)
                pre(j, 1, V_BANK[j], G_XO + 4 + j, ALPHA)
                layer_norm(ST + j, j, rows2, 1 if j < ST - 1 else 2)
                if j == 2:
                    ln2_lo(0)
                    ln2_lo(1)
                    w_split(N_FFN + 3, 3, 3)
            ln2_lo(2)
            ln2_lo(3)

            def ffn_segment(q, last):
                n, t = 12 * q + N_FFN, 8 * q + T_FFN

                def prm(i):
                    return par[:, bass.ds(16 * q + (C_FF + i), 1)]

                def conv(j):
                    dve.wait_ge(cg0_ready, 4 * q + j + 1)
                    v.scalar_tensor_tensor(cg[:, 1:S], ps[:, j % 2, 0:S - 1], prm(4 + j), cg[:, 1:S], ALU.mult,
                                           ALU.add).then_inc(cgtap, 1)
                    dve.wait_ge(cgtap, 4 * q + j + 1)
                    v.scalar_tensor_tensor(cg[:, 2:S], ps[:, j % 2, 0:S - 2], prm(8 + j), cg[:, 2:S], ALU.mult,
                                           ALU.add).then_inc(cg_ready, 1)

                def product(j):
                    dve.wait_ge(fg_ready, 4 * q + j + 1)
                    dve.wait_ge(tile_done, t + 2 * j + 2)
                    v.tensor_tensor(hf[:, :], fg[:, :], ps[:, 2 + j % 2, :], ALU.mult).then_inc(hf_ready, 1)

                def h_lo(j):
                    dve.wait_ge(hhi_ready, 4 * q + j + 1)
                    v.tensor_tensor(a_lo[:, j, :], hf[:, :], a_hi[:, j, :].bitcast(F32), ALU.subtract).then_inc(hlo_ready, 1)

                def accumulate(g):
                    tt, cols = g // 2, slice((g % 2) * HALF, (g % 2 + 1) * HALF)
                    dve.wait_ge(group_done, 8 * q + (G_FFN + g + 1))
                    v.tensor_tensor(resid[:, tt, cols], resid[:, tt, cols], ps[:, 4 + g % 4, :],
                                    ALU.add).then_inc(acc_ready, 1)

                w_split(n + 4, 0, 4)
                conv(0)
                w_split(n + 5, 1, 0)
                w_split(n + 6, 2, 1)
                product(0)
                w_split(n + 7, 3, 5)
                h_lo(0)
                conv(1)
                w_split(n + 8, 0, 2)
                w_split(n + 9, 1, 3)
                product(1)
                w_split(n + 10, 2, 6)
                h_lo(1)
                conv(2)
                w_split(n + 11, 3, 7)
                product(2)
                h_lo(2)
                conv(3)
                product(3)
                h_lo(3)
                if not last:
                    for g in range(8):
                        accumulate(g)
                        if g < 4:
                            w_split(n + 12 + g, g, g)
                else:
                    for tt in range(ST):
                        for h in range(2):
                            g = 2 * tt + h
                            accumulate(g)
                            dve.wait_ge(acc_ready, 8 * q + g + 1)
                            step(v.bn_stats(stats[:, tt, h, :], resid[:, tt, h * HALF:(h + 1) * HALF]))
                        layer_norm(2 * ST + tt, tt, rows3, 2)

            dve.wait_ge(scaled, ST)
            with dve.Fori(0, NSEG - 1) as q:
                ffn_segment(q, False)
            ffn_segment(NSEG - 1, True)

        @block.gpsimd
        def _(pool):
            nc.gpsimd.memset(ident[:, :], 0.0).then_inc(ident_ready, 1)
            pool.wait_ge(ident_ready, 1)
            nc.gpsimd.affine_select(out=ident[:, :], in_=ident[:, :], compare_op=ALU.not_equal, fill=1.0,
                                    base=0, pattern=[[-1, P]], channel_multiplier=1).then_inc(ident_ready, 1)
            with pool.Fori(0, KC) as c:
                pool.wait_ge(dec_ready, c + 1)
                nc.gpsimd.tensor_tensor(decsq[:, :], dec[:, :], dec[:, :], ALU.mult).then_inc(decsq_ready, 1)
            for t in range(ST):
                pool.wait_ge(turned, ST + t + 1)
                nc.gpsimd.tensor_scalar(resid[:, t, :], resid[:, t, :], ALPHA, 1.0, ALU.mult,
                                        ALU.mult).then_inc(scaled, 1)


PREP_STEPS = 21
LRU_AHEAD = 3
WARM = 12


def column_tiles(w, chunks):
    return [w[:, c * P:(c + 1) * P].reshape(KC, P, P).transpose(1, 0, 2).reshape(P, TW) for c in chunks]


def row_tiles(w):
    return [w[256 * j:256 * (j + 1), h * HALF:(h + 1) * HALF].reshape(2, P, HALF).transpose(1, 0, 2).reshape(P, TW)
            for h in range(2) for j in range(4)]


def lay_out(i):
    a = {k: np.asarray(x) for k, x in i.items()}
    w_in = a["w_in"][0]
    tiles = []
    for c in range(KC):
        tiles += column_tiles(w_in, [8 + c, c, 40 + c])
    tiles += column_tiles(a["w_lru_out"][0], range(KC))
    for c in range(KC):
        tiles += column_tiles(w_in, [24 + c, 32 + c, 16 + c, 48 + c])
    tiles += column_tiles(a["w_sc_out"][0], range(KC))
    tiles += row_tiles(a["w_mix_out"][0])
    tiles += column_tiles(a["w_k"][0], range(KC))
    tiles += column_tiles(a["w_q"][0], range(KC))
    tiles += row_tiles(a["w_v"][0])
    tiles += row_tiles(a["w_xo"][0])
    wg, wu, wd = a["w_ffn_gate"][0], a["w_ffn_up"][0], a["w_ffn_down"][0]
    for q in range(NSEG):
        gu = [t for j in range(SEG) for w in (wg, wu) for t in column_tiles(w, [SEG * q + j])]
        dn = [wd[(SEG * q + j) * P:(SEG * q + j + 1) * P, :] for j in range(SEG)]
        tiles += [gu[0], gu[1], gu[2], gu[3], dn[0], gu[4], gu[5], dn[1], gu[6], gu[7], dn[2], dn[3]]

    def chan(x):
        return x.reshape(-1, KC, P).transpose(2, 0, 1).reshape(P, -1)

    ffn = np.concatenate([a["ffn_conv_w"][0], a["ffn_conv_b"]], 0)
    ffn = ffn.reshape(4, NSEG, SEG, P).transpose(3, 1, 0, 2).reshape(P, -1)
    par = np.concatenate([chan(a["lru_conv_w"][0]), chan(a["lru_conv_b"]), chan(a["b_rgate"]), chan(a["b_igate"]),
                          chan(a["lru_lambda"]), chan(a["sc_conv_w"][0]), chan(a["b_merge"][0]), ffn], 1)
    x, mem = a["x"][0], a["mem"][0]
    return {
        "xt": x.T.reshape(4, 2, P, S).transpose(0, 2, 1, 3).reshape(4, P, 2 * S),
        "xtok": x,
        "memt": mem.T.reshape(4, 2, P, NM).transpose(0, 2, 1, 3).reshape(4, P, 2 * NM),
        "stream": np.stack(tiles),
        "gates": np.concatenate([a["w_rgate"][0], a["w_igate"][0]], 2),
        "params": par,
        "lnrows": np.concatenate([a[n] for n in ("ln1_g", "ln1_b", "ln2_g", "ln2_b", "ln3_g", "ln3_b")], 0),
    }


def kernel(**inputs):
    import concourse.bacc as bacc
    from concourse.bass_utils import run_bass_kernel_spmd

    nc = bacc.Bacc("TRN2", target_bir_lowering=False, num_devices=1)
    arrays = {f"in_{k}": np.ascontiguousarray(x) for k, x in lay_out(inputs).items()}
    args = [nc.dram_tensor(k, x.shape, mybir.dt.from_np(x.dtype), kind="ExternalInput").ap()
            for k, x in arrays.items()]
    out = nc.dram_tensor("out", (S, D), F32, kind="ExternalOutput").ap()
    build(nc, *args, out)
    r = run_bass_kernel_spmd(nc, [arrays], core_ids=[0])
    return r.results[0]["out"].reshape(1, S, D)
```
